# Optimizing a Trainium2 kernel written in Bass

```python
import math
import jax, jax.numpy as jnp
from jax import lax
import numpy as np

D_MODEL = 1024
BATCH = 1
SEQ = 512
DEPTH = 2

N_A_LAYERS = DEPTH // 2
N_B_LAYERS = DEPTH - N_A_LAYERS
HG_HEADS = 8
HG_DIM = D_MODEL // HG_HEADS
HG_CHUNK = 32
SW_Q_HEADS = 16
SW_KV_HEADS = 4
SW_HEAD_DIM = D_MODEL // SW_Q_HEADS
SW_GROUP = SW_Q_HEADS // SW_KV_HEADS
SW_WINDOW = 128
REL_BUCKETS = 32
REL_MAX_DIST = 128
FFN_DIM = 2816
CONV_WIDTH = 3
ALPHA = (2.0 * DEPTH) ** 0.25
BETA = (8.0 * DEPTH) ** -0.25
LN_EPS = 1e-5
RMS_EPS = 1e-6


def layer_norm(x, g, b):
    xf = x.astype(jnp.float32)
    mu = xf.mean(-1, keepdims=True)
    var = jnp.square(xf - mu).mean(-1, keepdims=True)
    y = (xf - mu) * lax.rsqrt(var + LN_EPS) * g.astype(jnp.float32) + b.astype(jnp.float32)
    return y.astype(x.dtype)

def hgrn2_chunkwise(q, k, v, log_f):
    B, S, H, Dk = q.shape
    Dv = v.shape[-1]
    n = S // HG_CHUNK

    def chunks(a):
        return a.reshape(B, n, HG_CHUNK, H, a.shape[-1]).transpose(1, 0, 3, 2, 4)

    qc, kc, vc = chunks(q), chunks(k), chunks(v)
    bc = jnp.cumsum(chunks(log_f), axis=3)
    causal = jnp.tril(jnp.ones((HG_CHUNK, HG_CHUNK), dtype=bool))[:, :, None]

    def step(state, inp):
        q_, k_, v_, b_ = inp
        o_inter = jnp.einsum('bhtk,bhkv->bhtv', q_ * jnp.exp(b_), state)
        diff = b_[:, :, :, None, :] - b_[:, :, None, :, :]
        decay = jnp.where(causal, jnp.exp(jnp.minimum(diff, 0.0)), 0.0)
        scores = jnp.einsum('bhtsk,bhsk->bhts', q_[:, :, :, None, :] * decay, k_)
        o = o_inter + jnp.einsum('bhts,bhsv->bhtv', scores, v_)
        b_last = b_[:, :, -1, :]
        k_dec = k_ * jnp.exp(b_last[:, :, None, :] - b_)
        state = jnp.exp(b_last)[..., None] * state + jnp.einsum('bhsk,bhsv->bhkv', k_dec, v_)
        return state, o

    state0 = jnp.zeros((B, H, Dk, Dv), jnp.float32)
    _, o = lax.scan(step, state0, (qc, kc, vc, bc))
    return o.transpose(1, 0, 3, 2, 4).reshape(B, S, H, Dv)

def hgrn2_mixer(h, w_in, lower_bound, g_norm_w, w_out):
    B, S, D = h.shape
    q, f, i, g = jnp.split(h @ w_in, 4, axis=-1)

    def heads(a):
        return a.reshape(B, S, HG_HEADS, HG_DIM).astype(jnp.float32)

    lb = lower_bound.astype(jnp.float32).reshape(HG_HEADS, HG_DIM)
    fg = lb + (1.0 - lb) * jax.nn.sigmoid(heads(f))
    o = hgrn2_chunkwise(jax.nn.silu(heads(q)), 1.0 - fg, heads(i), jnp.log(fg))
    o = o * lax.rsqrt(jnp.mean(jnp.square(o), -1, keepdims=True) + RMS_EPS)
    o = o * g_norm_w.astype(jnp.float32) * jax.nn.silu(heads(g))
    return o.reshape(B, S, D).astype(h.dtype) @ w_out

def t5_causal_bucket(dist):
    exact = REL_BUCKETS // 2
    d = jnp.maximum(dist, 1).astype(jnp.float32)
    log_b = exact + (jnp.log(d / exact) / math.log(REL_MAX_DIST / exact)
                     * (REL_BUCKETS - exact)).astype(jnp.int32)
    return jnp.where(dist < exact, dist, jnp.minimum(log_b, REL_BUCKETS - 1))

def banded_bias_and_mask(rel_table, n_blocks):
    t = jnp.arange(SW_WINDOW)[:, None] + SW_WINDOW
    s = jnp.arange(2 * SW_WINDOW)[None, :]
    dist = t - s
    bias = rel_table[t5_causal_bucket(jnp.maximum(dist, 0))].transpose(2, 0, 1)
    band = (dist >= 0) & (dist < SW_WINDOW)
    has_prev = (jnp.arange(n_blocks) > 0)[:, None, None]
    mask = band[None] & (has_prev | (s >= SW_WINDOW)[None])
    return bias, mask

def swa_sink_mixer(h, k, v, w_q, sinks, bias, mask, w_out):
    B, S, D = h.shape
    nb = S // SW_WINDOW
    q = (h @ w_q).reshape(B, nb, SW_WINDOW, SW_KV_HEADS, SW_GROUP, SW_HEAD_DIM)

    def with_prev(a):
        ab = a.reshape(B, nb, SW_WINDOW, SW_KV_HEADS, SW_HEAD_DIM)
        prev = jnp.pad(ab, ((0, 0), (1, 0), (0, 0), (0, 0), (0, 0)))[:, :-1]
        return jnp.concatenate([prev, ab], axis=2)

    kk, vv = with_prev(k), with_prev(v)
    scale = SW_HEAD_DIM ** -0.5
    logits = jnp.einsum('bntgrd,bnsgd->bngrts', q, kk).astype(jnp.float32) * scale
    logits = logits + bias.astype(jnp.float32).reshape(SW_KV_HEADS, SW_GROUP, SW_WINDOW, 2 * SW_WINDOW)
    logits = jnp.where(mask[None, :, None, None], logits, -jnp.inf)
    sink = sinks.astype(jnp.float32).reshape(1, 1, SW_KV_HEADS, SW_GROUP, 1)
    m = jnp.maximum(logits.max(-1), sink)
    p = jnp.exp(logits - m[..., None])
    denom = p.sum(-1) + jnp.exp(sink - m)
    o = jnp.einsum('bngrts,bnsgd->bntgrd', p, vv.astype(jnp.float32))
    o = o / jnp.moveaxis(denom, -1, 2)[..., None]
    return o.reshape(B, S, D).astype(h.dtype) @ w_out

def conv_ffn(h, w_in, conv_w, conv_b, w_out):
    u = h @ w_in
    C = u.shape[-1]
    u = lax.conv_general_dilated(u, conv_w[:, None, :], window_strides=(1,),
                                 padding=[(CONV_WIDTH - 1, 0)],
                                 dimension_numbers=('NWC', 'WIO', 'NWC'),
                                 feature_group_count=C) + conv_b
    a, b = jnp.split(u, 2, axis=-1)
    return (jax.nn.silu(a) * b) @ w_out

def first_inputs(seed: int = 0) -> dict:
    key = jax.random.key(seed)
    ks = jax.random.split(key, 24)
    D, F = D_MODEL, FFN_DIM
    kv_dim = SW_KV_HEADS * SW_HEAD_DIM
    nrm = jax.random.normal

    x = nrm(ks[0], (BATCH, SEQ, D), jnp.float32)

    hgrn_w_in = nrm(ks[1], (N_A_LAYERS, D, 4 * D), jnp.float32) * D ** -0.5
    hgrn_w_in = hgrn_w_in.at[..., 2 * D:3 * D].multiply(BETA)
    hgrn_lb_logits = nrm(ks[2], (N_A_LAYERS + 1, D), jnp.float32) * 0.5
    hgrn_gnorm_w = 1.0 + 0.02 * nrm(ks[3], (N_A_LAYERS, HG_DIM), jnp.float32)
    hgrn_w_out = nrm(ks[4], (N_A_LAYERS, D, D), jnp.float32) * D ** -0.5 * BETA

    swa_w_q = nrm(ks[5], (N_B_LAYERS, D, D), jnp.float32) * D ** -0.5
    swa_sinks = nrm(ks[6], (N_B_LAYERS, SW_Q_HEADS), jnp.float32) * 0.5
    swa_w_out = nrm(ks[7], (N_B_LAYERS, D, D), jnp.float32) * D ** -0.5 * BETA
    shared_w_kv = nrm(ks[8], (D, 2 * kv_dim), jnp.float32) * D ** -0.5
    shared_w_kv = shared_w_kv.at[:, kv_dim:].multiply(BETA)
    rel_bias = nrm(ks[9], (REL_BUCKETS, SW_Q_HEADS), jnp.float32) * 0.5

    ffn_w_in = nrm(ks[10], (DEPTH, D, 2 * F), jnp.float32) * D ** -0.5 * BETA
    ffn_conv_w = nrm(ks[11], (DEPTH, CONV_WIDTH, 2 * F), jnp.float32) * CONV_WIDTH ** -0.5
    ffn_conv_b = nrm(ks[12], (DEPTH, 2 * F), jnp.float32) * 0.02
    ffn_w_out = nrm(ks[13], (DEPTH, F, D), jnp.float32) * F ** -0.5 * BETA

    ln_mix_g = 1.0 + 0.02 * nrm(ks[14], (DEPTH, D), jnp.float32)
    ln_mix_b = 0.02 * nrm(ks[15], (DEPTH, D), jnp.float32)
    ln_ffn_g = 1.0 + 0.02 * nrm(ks[16], (DEPTH, D), jnp.float32)
    ln_ffn_b = 0.02 * nrm(ks[17], (DEPTH, D), jnp.float32)

    return {"x": x, "hgrn_w_in": hgrn_w_in, "hgrn_lb_logits": hgrn_lb_logits,
            "hgrn_gnorm_w": hgrn_gnorm_w, "hgrn_w_out": hgrn_w_out,
            "swa_w_q": swa_w_q, "swa_sinks": swa_sinks, "swa_w_out": swa_w_out,
            "shared_w_kv": shared_w_kv, "rel_bias": rel_bias,
            "ffn_w_in": ffn_w_in, "ffn_conv_w": ffn_conv_w, "ffn_conv_b": ffn_conv_b,
            "ffn_w_out": ffn_w_out, "ln_mix_g": ln_mix_g, "ln_mix_b": ln_mix_b,
            "ln_ffn_g": ln_ffn_g, "ln_ffn_b": ln_ffn_b}

def first_block(x, hgrn_w_in, hgrn_lb_logits, hgrn_gnorm_w, hgrn_w_out,
              swa_w_q, swa_sinks, swa_w_out, shared_w_kv, rel_bias,
              ffn_w_in, ffn_conv_w, ffn_conv_b, ffn_w_out,
              ln_mix_g, ln_mix_b, ln_ffn_g, ln_ffn_b):
    B, S, D = x.shape
    n_blocks = S // SW_WINDOW
    lower_bounds = jnp.cumsum(jax.nn.softmax(hgrn_lb_logits.astype(jnp.float32), axis=0), axis=0)
    bias, mask = banded_bias_and_mask(rel_bias, n_blocks)

    h = x
    k_shared = v_shared = None
    for layer in range(DEPTH):
        if layer < N_A_LAYERS:
            mix = hgrn2_mixer(h, hgrn_w_in[layer], lower_bounds[layer],
                              hgrn_gnorm_w[layer], hgrn_w_out[layer])
        else:
            j = layer - N_A_LAYERS
            mix = swa_sink_mixer(h, k_shared, v_shared, swa_w_q[j], swa_sinks[j],
                                 bias, mask, swa_w_out[j])
        h = layer_norm(ALPHA * h + mix, ln_mix_g[layer], ln_mix_b[layer])
        ff = conv_ffn(h, ffn_w_in[layer], ffn_conv_w[layer], ffn_conv_b[layer], ffn_w_out[layer])
        h = layer_norm(ALPHA * h + ff, ln_ffn_g[layer], ln_ffn_b[layer])
        if layer == N_A_LAYERS - 1:
            k_flat, v_flat = jnp.split(h @ shared_w_kv, 2, axis=-1)
            k_shared = k_flat.reshape(B, S, SW_KV_HEADS, SW_HEAD_DIM)
            v_shared = v_flat.reshape(B, S, SW_KV_HEADS, SW_HEAD_DIM)
    return h


DEPTH_2 = 1

HEAD_DIM = 64
MIX_WIDTH = D_MODEL
POOL_WIDTH = MIX_WIDTH // 4
POOL_GROUPS = 4
POOL_GROUP_DIM = POOL_WIDTH // POOL_GROUPS
POOL_WINDOWS = (2, 4, 8, 16)
FOX_WIDTH = MIX_WIDTH // 2
FOX_HEADS = FOX_WIDTH // HEAD_DIM
MEM_HEADS = 4
MEM_WIDTH = MEM_HEADS * HEAD_DIM
N_MEM = 256
Q_BLOCK = 128
EPS = 1e-6
SPLIT_SIZES = (POOL_WIDTH, POOL_WIDTH, FOX_WIDTH, FOX_WIDTH, FOX_WIDTH, FOX_HEADS, FOX_WIDTH, MEM_WIDTH, MEM_WIDTH)
IN_WIDTH = sum(SPLIT_SIZES)


def rms_norm(x, g):
    xf = x.astype(jnp.float32)
    y = xf * lax.rsqrt(jnp.mean(xf * xf, axis=-1, keepdims=True) + EPS)
    return (y * g.astype(jnp.float32)).astype(x.dtype)

def split_cols(proj):
    parts, off = [], 0
    for w in SPLIT_SIZES:
        parts.append(proj[..., off:off + w])
        off += w
    return parts

def to_heads(t, n_heads):
    b, s, _ = t.shape
    return t.reshape(b, s, n_heads, HEAD_DIM).transpose(0, 2, 1, 3)

def from_heads(t):
    b, h, s, d = t.shape
    return t.transpose(0, 2, 1, 3).reshape(b, s, h * d)

def pool_mixer(u, w_pool, scale):
    b, s, _ = u.shape
    uf = u.reshape(b, s, POOL_GROUPS, POOL_GROUP_DIM).astype(jnp.float32)
    csum = jnp.cumsum(uf, axis=1)
    pos = jnp.arange(1, s + 1, dtype=jnp.float32)
    pooled = []
    for g, w in enumerate(POOL_WINDOWS):
        cg = csum[:, :, g]
        lag = jnp.pad(cg, ((0, 0), (w, 0), (0, 0)))[:, :s]
        count = jnp.minimum(pos, float(w))
        pooled.append((cg - lag) / count[None, :, None])
    pooled = jnp.stack(pooled, axis=2)
    d = (pooled - uf).astype(u.dtype)
    y = jnp.einsum('bsgc,gce->bsge', d, w_pool).reshape(b, s, POOL_WIDTH)
    return y * scale

def fox_attention(q, k, v, logf):
    b, h, s, dh = q.shape
    n_blocks = s // Q_BLOCK
    F = jnp.cumsum(logf.astype(jnp.float32), axis=-1)
    qb = q.reshape(b, h, n_blocks, Q_BLOCK, dh).transpose(2, 0, 1, 3, 4)
    Fb = F.reshape(b, h, n_blocks, Q_BLOCK).transpose(2, 0, 1, 3)
    pos_k = jnp.arange(s)
    scale = 1.0 / math.sqrt(dh)

    def block(args):
        qi, Fi, i = args
        logits = jnp.einsum('bhqd,bhkd->bhqk', qi, k).astype(jnp.float32) * scale
        logits = logits + Fi[..., None] - F[:, :, None, :]
        pos_q = i * Q_BLOCK + jnp.arange(Q_BLOCK)
        causal = pos_k[None, :] <= pos_q[:, None]
        logits = jnp.where(causal, logits, -1e30)
        p = jax.nn.softmax(logits, axis=-1)
        return jnp.einsum('bhqk,bhkd->bhqd', p.astype(v.dtype), v)

    out = lax.map(block, (qb, Fb, jnp.arange(n_blocks)))
    return out.transpose(1, 2, 0, 3, 4).reshape(b, h, s, dh)

def memory_attention(q, k, v):
    scale = 1.0 / math.sqrt(q.shape[-1])
    logits = jnp.einsum('bhqd,bhmd->bhqm', q, k).astype(jnp.float32) * scale
    p = jax.nn.softmax(logits, axis=-1)
    return jnp.einsum('bhqm,bhmd->bhqd', p.astype(v.dtype), v)

def second_inputs(seed: int = 0) -> dict:
    key = jax.random.key(seed)
    ks = jax.random.split(key, 16)
    f32 = jnp.float32
    x = jax.random.normal(ks[0], (BATCH, SEQ, D_MODEL), f32)
    mem = jax.random.normal(ks[1], (BATCH, N_MEM, D_MODEL), f32)
    norm_g = 1.0 + 0.02 * jax.random.normal(ks[2], (DEPTH_2, D_MODEL), f32)
    w_in = jax.random.normal(ks[3], (DEPTH_2, D_MODEL, IN_WIDTH), f32) * D_MODEL ** -0.5
    b_f = 1.0 + 4.0 * jax.random.uniform(ks[4], (DEPTH_2, FOX_HEADS), f32)
    w_pool = jax.random.normal(ks[5], (DEPTH_2, POOL_GROUPS, POOL_GROUP_DIM, POOL_GROUP_DIM), f32) * POOL_GROUP_DIM ** -0.5
    pool_scale = 1.0 + 0.02 * jax.random.normal(ks[6], (DEPTH_2, POOL_WIDTH), f32)
    fox_q_g = 1.0 + 0.02 * jax.random.normal(ks[7], (DEPTH_2, HEAD_DIM), f32)
    fox_k_g = 1.0 + 0.02 * jax.random.normal(ks[8], (DEPTH_2, HEAD_DIM), f32)
    mem_norm_g = 1.0 + 0.02 * jax.random.normal(ks[9], (DEPTH_2, D_MODEL), f32)
    w_mem_kv = jax.random.normal(ks[10], (DEPTH_2, D_MODEL, 2 * MEM_WIDTH), f32) * D_MODEL ** -0.5
    mem_q_g = 1.0 + 0.02 * jax.random.normal(ks[11], (DEPTH_2, HEAD_DIM), f32)
    mem_k_g = 1.0 + 0.02 * jax.random.normal(ks[12], (DEPTH_2, HEAD_DIM), f32)
    w_out = jax.random.normal(ks[13], (DEPTH_2, MIX_WIDTH, D_MODEL), f32) * MIX_WIDTH ** -0.5
    return {"x": x, "mem": mem, "norm_g": norm_g, "w_in": w_in, "b_f": b_f,
            "w_pool": w_pool, "pool_scale": pool_scale, "fox_q_g": fox_q_g,
            "fox_k_g": fox_k_g, "mem_norm_g": mem_norm_g, "w_mem_kv": w_mem_kv,
            "mem_q_g": mem_q_g, "mem_k_g": mem_k_g, "w_out": w_out}

def second_block(x, mem, norm_g, w_in, b_f, w_pool, pool_scale, fox_q_g, fox_k_g,
              mem_norm_g, w_mem_kv, mem_q_g, mem_k_g, w_out):
    for l in range(DEPTH_2):
        h = rms_norm(x, norm_g[l])
        proj = jnp.einsum('bsd,de->bse', h, w_in[l])
        u_a, g_a, q_b, k_b, v_b, f_b, g_b, q_m, g_m = split_cols(proj)

        y_a = pool_mixer(u_a, w_pool[l], pool_scale[l])

        q = rms_norm(to_heads(q_b, FOX_HEADS), fox_q_g[l])
        k = rms_norm(to_heads(k_b, FOX_HEADS), fox_k_g[l])
        v = to_heads(v_b, FOX_HEADS)
        logf = jax.nn.log_sigmoid((f_b + b_f[l]).astype(jnp.float32)).transpose(0, 2, 1)
        y_b = from_heads(fox_attention(q, k, v, logf))

        mem_n = rms_norm(mem, mem_norm_g[l])
        kv = jnp.einsum('bmd,de->bme', mem_n, w_mem_kv[l])
        k_m = rms_norm(to_heads(kv[..., :MEM_WIDTH], MEM_HEADS), mem_k_g[l])
        v_m = to_heads(kv[..., MEM_WIDTH:], MEM_HEADS)
        q_mh = rms_norm(to_heads(q_m, MEM_HEADS), mem_q_g[l])
        y_m = from_heads(memory_attention(q_mh, k_m, v_m))

        mixed = jnp.concatenate([y_a * jax.nn.silu(g_a),
                                 y_b * jax.nn.silu(g_b),
                                 y_m * jax.nn.silu(g_m)], axis=-1)
        x = x + jnp.einsum('bse,ed->bsd', mixed, w_out[l])
    return x


def setup_inputs(seed=0):
    out = dict(first_inputs(seed))
    for name, value in second_inputs(seed + 1).items():
        if name != "x":
            out[name + "_2"] = value
    return out


def reference(
    x, hgrn_w_in, hgrn_lb_logits, hgrn_gnorm_w, hgrn_w_out, swa_w_q, swa_sinks, swa_w_out,
    shared_w_kv, rel_bias, ffn_w_in, ffn_conv_w, ffn_conv_b, ffn_w_out, ln_mix_g, ln_mix_b,
    ln_ffn_g, ln_ffn_b, mem_2, norm_g_2, w_in_2, b_f_2, w_pool_2, pool_scale_2, fox_q_g_2,
    fox_k_g_2, mem_norm_g_2, w_mem_kv_2, mem_q_g_2, mem_k_g_2, w_out_2,
):
    x = first_block(
        x, hgrn_w_in, hgrn_lb_logits, hgrn_gnorm_w, hgrn_w_out, swa_w_q, swa_sinks, swa_w_out,
        shared_w_kv, rel_bias, ffn_w_in, ffn_conv_w, ffn_conv_b, ffn_w_out, ln_mix_g, ln_mix_b,
        ln_ffn_g, ln_ffn_b,
    )
    return second_block(
        x, mem_2, norm_g_2, w_in_2, b_f_2, w_pool_2, pool_scale_2, fox_q_g_2, fox_k_g_2,
        mem_norm_g_2, w_mem_kv_2, mem_q_g_2, mem_k_g_2, w_out_2,
    )


_drawn_inputs = setup_inputs


def setup_inputs(seed=0):
    import zlib

    import numpy as np

    out = dict(_drawn_inputs(seed))
    spreads = {}
    factors = {'hgrn_lb_logits': 4.292,
     'hgrn_gnorm_w': 8.0,
     'swa_sinks': 8.0,
     'rel_bias': 4.137,
     'ffn_conv_b': 8.0,
     'norm_g_2': 6.59,
     'pool_scale_2': 8.0,
     'fox_q_g_2': 8.0,
     'fox_k_g_2': 8.0,
     'mem_norm_g_2': 8.0,
     'mem_q_g_2': 8.0,
     'mem_k_g_2': 8.0}
    for name, (base, spread) in spreads.items():
        noise = np.random.default_rng([zlib.crc32(name.encode()), seed]).standard_normal(out[name].shape)
        drawn = base * np.exp(spread * noise) if base else spread * noise
        out[name] = __import__('jax').numpy.asarray(drawn.astype(out[name].dtype))
    for name, factor in factors.items():
        out[name] = (out[name] * factor).astype(out[name].dtype)
    return out
```

```python
from contextlib import ExitStack

import numpy as np

import concourse.bass as bass
from concourse import mybir

F32 = mybir.dt.float32
F32R = mybir.dt.float32r
U32 = mybir.dt.uint32
ALU = mybir.AluOpType
ACT = mybir.ActivationFunctionType
AX_X = mybir.AxisListType.X

P = 128
D = 1024
KB = D // P
T = 512
TT = T // P
FFN = 2816
FB = FFN // P
DEPTH = 2
HEADS = 8
LEVELS = 7
SWH = 16
MEM = 256
ALPHA = (2.0 * DEPTH) ** 0.25
LN_EPS = 1e-5
RMS_EPS = 1e-6
NEG = -1e30
TINY = 2.0 ** -64
SCALE = 64 ** -0.5
BUCKETS = 32
POOL_WINDOWS = (2, 4, 8, 16)

N_HG = 0
N_HO = N_HG + 16
N_F0 = N_HO + 4
N_D0 = N_F0 + FB
N_KV = N_D0 + FB // 2
N_SQ = N_KV + 2
N_SO = N_SQ + 4
N_F1 = N_SO + 4
N_D1 = N_F1 + FB
N_MEM = N_D1 + FB // 2
N_FG = N_MEM + 2
N_UA = N_FG + 1
N_QM = N_UA + 1
N_GA = N_QM + 1
N_GM = N_GA + 1
N_FX = N_GM + 1
N_OUT = N_FX + 8
N_ALL = N_OUT + 4

PARAMS = [("lb", 16), ("gnorm", 1), ("conv_w", 264), ("conv_b", 88), ("mix_g", 16), ("mix_b", 16),
          ("ffn_g", 16), ("ffn_b", 16), ("norm_g", 8), ("mem_g", 8), ("pool_scale", 2),
          ("fox_qg", 1), ("fox_kg", 1), ("mem_qg", 1), ("mem_kg", 1), ("forget_b", 1)]
CONSTS = [("ident", P), ("mean", P), ("mean64", P), ("causal", P), ("carry", T), ("eps_ln", 1),
          ("eps_rms", 1), ("one", 1), ("inv_count", 2 * T)]


def columns(table):
    at, out = 0, {}
    for name, n in table:
        out[name] = (at, at + n)
        at += n
    return out, at


PCOL, NPAR = columns(PARAMS)
CCOL, NCON = columns(CONSTS)


def build(nc, stream, x_t, mem_t, params, consts, masks, sinks, rel_in, w_pool, out):
    bias_rows = nc.dram_tensor("bias_rows", (P, SWH, 2 * P), F32).ap()
    forget_rows = nc.dram_tensor("forget_rows", (8, T), F32).ap()
    bias_toeplitz = bass.AP(bias_rows.tensor, 0, [[SWH * 2 * P - 1, P], [2 * P, SWH], [1, 2 * P]])
    forget_bcast = bass.AP(forget_rows.tensor, 0, [[0, P], [T, 8], [1, T]])
    sinks_bcast = bass.AP(sinks.tensor, 0, [[0, P], [1, SWH]])

    with ExitStack() as ctx:
        def sb(name, shape, dt=F32, scope=ctx):
            return scope.enter_context(nc.sbuf_tensor(name, shape, dt))

        def sem(name):
            return ctx.enter_context(nc.semaphore(name))

        H = sb("H", [P, KB, T])
        with ExitStack() as s:
            PL2 = sb("PL2", [P, 3, 2, T], F32, s)
            PT2 = sb("PT2", [P, 2, 2, T], F32, s)
            TO = sb("TO", [P, T], F32, s)
        AH = sb("AH", [P, KB, T], F32R)
        AL = sb("AL", [P, KB, T], F32R)
        RAW = [sb(f"RAW{s}", [P, 2048]) for s in range(2)]
        WH = [sb(f"WH{s}", [P, 2048], F32R) for s in range(2)]
        WL = [sb(f"WL{s}", [P, 2048], F32R) for s in range(2)]
        PAR = sb("PAR", [P, NPAR])
        CON = sb("CON", [P, NCON])
        MASK = sb("MASK", [P, 8, P])
        SINK = sb("SINK", [P, SWH])
        LB = sb("LB", [P, 4, 8])
        SMALL = sb("SMALL", [P, 4, 3, 4])
        PAD = sb("PAD", [P, 1])
        par = {k: PAR[:, a:b] for k, (a, b) in PCOL.items()}
        con = {k: CON[:, a:b] for k, (a, b) in CCOL.items()}
        CONVW = par["conv_w"].rearrange("p (l t a j) -> p l t a j", l=2, t=3, a=2)
        CONVB = par["conv_b"].rearrange("p (l a j) -> p l a j", l=2, a=2)
        NMAX, SUMS, SNK, RDEN = (SMALL[:, i] for i in range(4))

        with ExitStack() as s:
            sb("OH_HEAD", [P, 2, T], F32, s)
            SQH = sb("SQH", [P, 2, T], F32, s)
            RH = sb("RH", [P, 2, T], F32, s)
            PU = sb("PU", [P, 2, T], F32, s)
            sb("OL_HEAD", [P, 2, T], F32, s)
            PS = sb("PS", [P, 2, T], F32, s)
            PD = sb("PD", [P, 2, T], F32, s)
            TP = sb("TP", [P, T], F32, s)
            WP = sb("WP", [P, 2, P], F32, s)
        with ExitStack() as s:
            OH = sb("OH", [P, KB, T], F32R, s)
            OL = sb("OL", [P, KB, T], F32R, s)
            with ExitStack() as s1:
                one = lambda name: sb(name, [P, 2, T], F32, s1)
                E1, KK, BB, EB, QQ, QI, KD = (one(n) for n in ("E1", "KK", "BB", "EB", "QQ", "QI", "KD"))
                DD = sb("DD", [P, 2, 2, T], F32, s1)
                QT = sb("QT", [P, 2, 2, T], F32, s1)
                KT_ = sb("KT_", [P, 2, 2, T], F32, s1)
                SS = sb("SS", [P, 2, TT, P], F32, s1)
                VV = sb("VV", [P, TT, 2 * P], F32, s1)
            with ExitStack() as s1:
                REL = sb("REL", [BUCKETS, SWH + 2 * P], F32, s1)
                ROWS = sb("ROWS", [SWH, 2 * P], F32, s1)
                ROWM = sb("ROWM", [SWH, 2 * P], F32, s1)
            with ExitStack() as s1:
                BIAS = sb("BIAS", [P, SWH, 2 * P], F32, s1)
                KT = sb("KT", [P, 2, T], F32, s1)
                VT = sb("VT", [P, TT, 2 * P], F32, s1)
                KC = sb("KC", [P, T], F32, s1)
                VC = sb("VC", [P, TT, P], F32, s1)
                QB = sb("QB", [P, 4, T], F32, s1)
                PL = sb("PL", [P, 3, 4, 2 * P], F32, s1)
                PT = sb("PT", [P, 2, 8, P], F32, s1)
            with ExitStack() as s1:
                MT = sb("MT", [P, KB, MEM], F32, s1)
                MH = sb("MH", [P, KB, MEM], F32R, s1)
                ML = sb("ML", [P, KB, MEM], F32R, s1)
                TN = sb("TN", [P, KB, T], F32, s1)
            with ExitStack() as s1:
                FBC = sb("FBC", [P, 8, T], F32, s1)
                KM = sb("KM", [P, 2, MEM], F32, s1)
                VM = sb("VM", [P, 2, MEM], F32, s1)
                QKN = sb("QKN", [P, 4, 2, T], F32, s1)
                VF = sb("VF", [P, 4, TT, P], F32, s1)
                SG = sb("SG", [P, KB, T], F32, s1)
                QMN = sb("QMN", [P, 2, T], F32, s1)
                FG_ = SG[0:8, 2:6]
        with ExitStack() as s:
            GH = sb("GH", [P, FB, T], F32R, s)
            GL = sb("GL", [P, FB, T], F32R, s)
            with ExitStack() as s1:
                CA = sb("CA", [P, 2, T], F32, s1)
                CB = sb("CB", [P, 2, T], F32, s1)
            with ExitStack() as s1:
                SQ = sb("SQ", [P, 2, T], F32, s1)
                MEAN = sb("MEAN", [P, T], F32, s1)
                VAR = sb("VAR", [P, T], F32, s1)

        bank = [ctx.enter_context(nc.psum_tensor(f"pair{i}", [P, 2, T], F32)) for i in range(4)]

        def bk(i):
            return bank[i // 2][:, i % 2]

        w_loaded = [sem("w_loaded0"), sem("w_loaded1")]
        w_hi, w_lo, w_used = sem("w_hi"), sem("w_lo"), sem("w_used")
        consts_in, rel_loaded, mem_loaded = sem("consts_in"), sem("rel_loaded"), sem("mem_loaded")
        x_loaded = [sem("x_loaded0"), sem("x_loaded1")]
        a_ready, ah_ready, o_ready, g_ready = sem("a_ready"), sem("ah_ready"), sem("o_ready"), sem("g_ready")
        m_ready, mh_ready = sem("m_ready"), sem("mh_ready")
        rel_mm, rows_made, rows_stored, bias_loaded = (sem(n) for n in ("rel_mm", "rows_made", "rows_stored", "bias_loaded"))
        lb_shifted, lb_exp = sem("lb_shifted"), sem("lb_exp")
        f_soft, f_logsig, f_sig, fg_made, lf_made, b_made = (sem(n) for n in ("f_soft", "f_logsig", "f_sig", "fg_made", "lf_made", "b_made"))
        q_soft, q_logsig, q_sig, q_read = (sem(n) for n in ("q_soft", "q_logsig", "q_sig", "q_read"))
        eb_exp, kd_shifted, kd_exp, kd_made = (sem(n) for n in ("eb_exp", "kd_shifted", "kd_exp", "kd_made"))
        level_shifted, level_exp, level_made, level_mm, level_picked = (
            sem(n) for n in ("level_shifted", "level_exp", "level_made", "level_mm", "level_picked"))
        v_copied = sem("v_copied")
        gate_soft, gate_logsig, gate_sig, gate_read = (sem(n) for n in ("gate_soft", "gate_logsig", "gate_sig", "gate_read"))
        kd_turned, kd_copied, kv_mm, state_made, o_mm, o_squared, o_summed, o_rstd = (
            sem(n) for n in ("kd_turned", "kd_copied", "kv_mm", "state_made", "o_mm", "o_squared", "o_summed", "o_rstd"))
        r_done, y_ready, y_squared, y_summed, var_made, rstd_made, normed = (
            sem(n) for n in ("r_done", "y_ready", "y_squared", "y_summed", "var_made", "rstd_made", "normed"))
        h_ready, h_squared, h_summed, h_rstd, t_made = (sem(n) for n in ("h_ready", "h_squared", "h_summed", "h_rstd", "t_made"))
        m_squared, m_summed, m_rstd, tm_made = (sem(n) for n in ("m_squared", "m_summed", "m_rstd", "tm_made"))
        u_read, a_silu = sem("u_read"), sem("a_silu")
        kv_copied, qb_copied, group_copied = sem("kv_copied"), sem("qb_copied"), sem("group_copied")
        s_mm, l_ready, p_exp, p_ready, p_turned, pt_ready, pv_mm = (
            sem(n) for n in ("s_mm", "l_ready", "p_exp", "p_ready", "p_turned", "pt_ready", "pv_mm"))
        n_squared, n_summed, n_rstd, n_made = (sem(n) for n in ("n_squared", "n_summed", "n_rstd", "n_made"))
        fox_v, vm_copied = sem("fox_v"), sem("vm_copied")
        sg_made, pu_read, pool_w_loaded = sem("sg_made"), sem("pu_read"), sem("pool_w_loaded")
        z_abs, z_exp, f_made, f_stored, f_bcast = (sem(n) for n in ("z_abs", "z_exp", "f_made", "f_stored", "f_bcast"))
        pooled, pool_mm = sem("pooled"), sem("pool_mm")
        out_ready, stored = sem("out_ready"), sem("stored")

        def wcols(slot):
            return (WH[slot][:, :].rearrange("p (k c) -> p k c", k=8), WL[slot][:, :].rearrange("p (k c) -> p k c", k=8))

        def wrows(slot):
            return (WH[slot][:, :].rearrange("p (k c) -> p k c", k=2), WL[slot][:, :].rearrange("p (k c) -> p k c", k=2))

        def halves(ap, m):
            return ap.rearrange("p h (n w m) -> p (h n) w m", w=2, m=m)

        SW_UNITS = [("sw", b, (2 * h, 2 * h + 1)) for b in range(4) for h in range(2)]
        LAST_UNITS = [("fox", j, (n,)) for j in range(4) for n in range(TT)] + \
                     [("mem", 4 + b, (2 * h, 2 * h + 1)) for b in range(2) for h in range(2)]
        U_LAST = 2 * len(SW_UNITS)

        def rows_of(unit, buf, slot):
            kind, _, tiles = unit
            if kind == "fox":
                return buf[:, slot, :, 0:(tiles[0] + 1) * P]
            if kind == "mem":
                return buf[:, slot].rearrange("p x (t s) -> p x t s", t=2)
            return buf[:, slot].rearrange("p (x t) s -> p x t s", t=2)

        def per_row(unit, small, slot):
            if unit[0] == "fox":
                return small[:, slot, 0:2]
            return small[:, slot].rearrange("p (x t) -> p x t", t=2)

        def ends_pair(units, i):
            return i >= 0 and (i + 1 == len(units) or units[i + 1][1] != units[i][1])

        block = ctx.enter_context(nc.Block())

        @block.sync
        def _(sp):
            def load(n, slot):
                sp.dma_start(RAW[slot][:, :], stream[n]).then_inc(w_loaded[slot], 16)

            for half in range(2):
                sp.dma_start(H[:, 4 * half:4 * half + 4], x_t[:, 4 * half:4 * half + 4]).then_inc(x_loaded[half], 16)
                load(half, half)
            with sp.Fori(0, (N_ALL - 2) // 2) as i:
                for slot in range(2):
                    sp.wait_ge(w_lo, 2 * i + slot + 1)
                    load(2 * i + (slot + 2), slot)
            if N_ALL % 2:
                sp.wait_ge(w_lo, N_ALL - 2)
                load(N_ALL - 1, (N_ALL - 1) % 2)

        @block.gpsimd
        def _(pool):
            def split_lo(n, slot):
                pool.wait_ge(w_hi, n + 1)
                pool.tensor_tensor(WL[slot][:, :], RAW[slot][:, :], WH[slot][:, :].bitcast(F32),
                                   ALU.subtract).then_inc(w_lo, 1)

            with pool.Fori(0, N_ALL // 2) as i:
                for slot in range(2):
                    split_lo(2 * i + slot, slot)
            if N_ALL % 2:
                split_lo(N_ALL - 1, (N_ALL - 1) % 2)

        @block.tensor
        def _(pe):
            def three(out_, wh, wl, xh, xl, start, stop):
                pe.matmul(out_, wh, xh, start=start, stop=False)
                pe.matmul(out_, wh, xl, start=False, stop=False)
                return pe.matmul(out_, wl, xh, start=False, stop=stop)

            def col_chunk(n, slot, banks, xh, xl, ms=(0, 1), ready=None, w=T, last=True, mid=None):
                pe.wait_ge(w_lo, n + 1)
                wh, wl = wcols(slot)
                for k in range(KB):
                    if mid and k == 3:
                        mid()
                    if ready:
                        pe.wait_ge(ready[0], ready[1] + k + 1)
                    for m in ms:
                        mm = three(banks[m][:, 0:w], wh[:, k, m * P:m * P + P], wl[:, k, m * P:m * P + P],
                                   xh[:, k], xl[:, k], k == 0, k == KB - 1)
                if last:
                    mm.then_inc(w_used, 1)
                return mm

            def tok_chunk(n, slot, outs, c0, c1, xh, xl, last=True, mid=None):
                pe.wait_ge(w_lo, n + 1)
                wh, wl = wcols(slot)
                for t, o in enumerate(outs):
                    if mid and t == 2:
                        mid()
                    for k in range(KB):
                        mm = three(o, xh[:, k, t * P:t * P + P], xl[:, k, t * P:t * P + P],
                                   wh[:, k, c0:c1], wl[:, k, c0:c1], k == 0, k == KB - 1)
                if last:
                    mm.then_inc(w_used, 1)

            def row_chunk(n, slot, j, xh, xl, first, last):
                pe.wait_ge(w_lo, n + 1)
                wh, wl = wrows(slot)
                for m in range(8):
                    for k in range(2):
                        xk = bass.ds(2 * j + k, 1)
                        mm = three(bk(m), wh[:, k, m * P:m * P + P], wl[:, k, m * P:m * P + P],
                                   xh[:, xk].squeeze(1), xl[:, xk].squeeze(1), first and k == 0, last and k == 1)
                    if last and m < 7:
                        mm.then_inc(r_done, 1)
                mm.then_inc(w_used, 1)

            def layer_sums(idx):
                for m in range(KB):
                    pe.wait_ge(y_ready, 8 * idx + max(m + 1, 2))
                    pe.matmul(bk(0), con["mean"], H[:, m], start=m == 0, stop=m == 7)
                    pe.wait_ge(y_squared, 8 * idx + m + 1)
                    pe.matmul(bk(1), con["mean"], SQ[:, m % 2], start=m == 0, stop=m == 7).then_inc(y_summed, 1)

            pe.wait_ge(rel_loaded, 32)
            pe.matmul(bk(7)[0:SWH, 0:2 * P], REL[:, 0:SWH], REL[:, SWH:SWH + 2 * P], start=True, stop=True).then_inc(rel_mm, 1)

            def project_f(it, first=False):
                pe.wait_ge(v_copied, it)
                col_chunk(N_HG + 4 * it, 0, (bk(0), bk(1)), AH, AL, ready=(a_ready, 0) if first else None)

            def project_q(it):
                pe.wait_ge(gate_read, it)
                col_chunk(N_HG + 1 + 4 * it, 1, (bk(2), bk(3)), AH, AL)

            def hgrn(it, last):
                n = N_HG + 4 * it
                pe.wait_ge(f_logsig, it + 1)
                tok_chunk(n + 2, 0, [bk(t // 2)[:, 256 * (t % 2):256 * (t % 2) + 256] for t in range(TT)], 0, 256, AH, AL)

                def level(lv):
                    s = lv % 2
                    if lv == 0:
                        pe.wait_ge(o_ready, 2 * it)
                    if lv >= 2:
                        pe.wait_ge(level_picked, 8 * it + lv - 1)
                    if lv < LEVELS:
                        pe.wait_ge(level_made, 7 * it + lv + 1)
                    for h in range(2):
                        for c in range(TT):
                            cs = slice(c * P, c * P + P)
                            k_, q_ = (KT_[:, s, h, cs], QT[:, s, h, cs]) if lv < LEVELS else (KK[:, h, cs], QQ[:, h, cs])
                            mm = pe.matmul(bk(4 + 2 * s + h)[:, cs], k_, q_, start=True, stop=True)
                    mm.then_inc(level_mm, 1)

                for lv in range(4):
                    level(lv)
                pe.wait_ge(q_read, it + 1)
                col_chunk(n + 3, 1, (bk(2), bk(3)), AH, AL)
                for lv in range(4, 8):
                    level(lv)
                pe.wait_ge(kd_made, it + 1)
                pe.wait_ge(level_picked, 8 * it + 7)
                for h in range(2):
                    for c in range(TT - 1):
                        mm = pe.transpose(bk(4 + h)[:, c * P:c * P + P], KD[:, h, c * P:c * P + P], con["ident"])
                mm.then_inc(kd_turned, 1)
                if not last:
                    project_f(it + 1)
                pe.wait_ge(kd_copied, it + 1)
                pe.wait_ge(v_copied, it + 1)
                pe.wait_ge(level_picked, 8 * it + 8)
                for h in range(2):
                    for c in range(TT - 1):
                        mm = pe.matmul(bk(6 + h)[:, c * P:c * P + P], QT[:, 0, h, c * P:c * P + P],
                                       VV[:, c, h * P:h * P + P], start=True, stop=True)
                mm.then_inc(kv_mm, 1)
                pe.wait_ge(state_made, it + 1)
                for h in range(2):
                    for c in range(TT):
                        cs = slice(c * P, c * P + P)
                        if c:
                            pe.matmul(bk(4 + h)[:, cs], BB[:, h, (c - 1) * P:c * P], QI[:, h, cs], start=True, stop=False)
                        mm = pe.matmul(bk(4 + h)[:, cs], VV[:, c, h * P:h * P + P], SS[:, h, c], start=c == 0, stop=True)
                mm.then_inc(o_mm, 1)
                pe.wait_ge(o_squared, it + 1)
                for h in range(2):
                    mm = pe.matmul(bk(6 + h), con["mean"], DD[:, 0, h], start=True, stop=True)
                mm.then_inc(o_summed, 1)
                if not last:
                    project_q(it + 1)

            pe.wait_ge(consts_in, 80)
            project_f(0, first=True)
            project_q(0)
            with pe.Fori(0, 3) as it:
                hgrn(it, False)
            hgrn(3, True)

            def out_projection(n0, slot0, j_ready, base):
                pe.wait_ge(j_ready, base + 8)
                for j in range(4):
                    row_chunk(n0 + j, (slot0 + j) % 2, j, OH, OL, j == 0, j == 3)

            def ffn(layer, n_in, n_down, a_base):
                s0 = n_in % 2

                def pair(j, first):
                    n = n_in + 2 * j
                    if not first:
                        pe.wait_ge(u_read, FB * layer + 2 * j - 1)
                    col_chunk(n, s0, (bk(0), bk(1)), AH, AL, ready=(a_ready, a_base) if first else None)
                    if not first:
                        pe.wait_ge(u_read, FB * layer + 2 * j)
                    col_chunk(n + 1, 1 - s0, (bk(2), bk(3)), AH, AL)

                pair(0, True)
                with pe.Fori(1, FB // 2) as j:
                    pair(j, False)
                s0 = n_down % 2
                pe.wait_ge(u_read, FB * (layer + 1))

                def down(j, s, first=False, last=False):
                    pe.wait_ge(g_ready, 11 * layer + j + 1)
                    row_chunk(n_down + j, s, j, GH, GL, first, last)

                down(0, s0, first=True)
                with pe.Fori(0, 4) as i:
                    down(2 * i + 1, 1 - s0)
                    down(2 * i + 2, s0)
                down(9, 1 - s0)
                down(10, s0, last=True)

            pe.wait_ge(v_copied, 4)
            pe.wait_ge(gate_read, 4)
            out_projection(N_HO, N_HO % 2, o_ready, 0)
            layer_sums(0)
            ffn(0, N_F0, N_D0, 8)
            layer_sums(1)

            def attend(u0, units, query, key, value, PL, PT, pair_free):
                def keys_of(unit, n):
                    return {"sw": (max(n - 1, 0), min(n + 1, 2)), "fox": (0, n + 1), "mem": (0, 2)}[unit[0]]

                def score(i):
                    kind, b, tiles = units[i]
                    s = i % 2
                    if i >= 2:
                        pe.wait_ge(l_ready, u0 + i - 1)
                    for t, n in enumerate(tiles):
                        k0, nk = keys_of(units[i], n)
                        for x in range(2):
                            if kind == "fox":
                                o = bk(2 * s + x)[:, 0:nk * P]
                            else:
                                o = bk(2 * s + x)[:, 256 * t + (2 - nk) * P:256 * t + 256]
                            mm = pe.matmul(o, query(b, n)[64 * x:64 * x + 64], key(b, k0, nk)[64 * x:64 * x + 64],
                                           start=True, stop=True)
                    mm.then_inc(s_mm, 1)

                def turn(i):
                    kind, b, tiles = units[i]
                    rows = rows_of(units[i], PL, i % 3)
                    pe.wait_ge(p_ready, u0 + i + 1)
                    pe.wait_ge(pt_ready, u0 + i)
                    for t in range(len(tiles)):
                        for x in range(2):
                            src = rows[:, x] if kind == "fox" else rows[:, x, t]
                            for kb in range(tiles[0] + 1 if kind == "fox" else 2):
                                at = x * 4 + 2 * t + kb
                                mm = pe.transpose(bk(4 + at // 4)[:, at % 4 * P:at % 4 * P + P],
                                                  src[:, kb * P:kb * P + P], con["ident"])
                    mm.then_inc(p_turned, 1)

                def weigh(i):
                    kind, b, tiles = units[i]
                    pe.wait_ge(pt_ready, u0 + i + 1)
                    if ends_pair(units, i - 1) and b >= 2:
                        pe.wait_ge(o_ready, pair_free + b - 1)
                    for t, n in enumerate(tiles):
                        k0, nk = keys_of(units[i], n)
                        for x in range(2):
                            for kb in range(nk):
                                at = x * 4 + kb if kind == "fox" else x * 4 + t * 2 + kb + 2 - nk
                                mm = pe.matmul(bk(6 + b % 2)[64 * x:64 * x + 64, n * P:n * P + P], value(b, k0 + kb, x),
                                               PT[:, i % 2, at], start=kb == 0, stop=kb == nk - 1)
                    mm.then_inc(pv_mm, 1)

                score(0)
                score(1)
                for i in range(len(units)):
                    if i + 2 < len(units):
                        score(i + 2)
                    turn(i)
                    if i:
                        weigh(i - 1)
                weigh(len(units) - 1)

            s0 = N_KV % 2
            col_chunk(N_KV, s0, (bk(2), bk(3)), AH, AL, ready=(a_ready, 16))
            tok_chunk(N_KV + 1, 1 - s0, [bk(4 + t // 2)[:, 256 * (t % 2):256 * (t % 2) + 256] for t in range(TT)], 0, 256, AH, AL)

            pe.wait_ge(kv_copied, 2)
            s0 = N_SQ % 2
            with pe.Fori(0, 2) as it:
                pe.wait_ge(l_ready, 8 * it)
                col_chunk(N_SQ + 2 * it, s0, (bk(0), bk(1)), AH, AL)
                col_chunk(N_SQ + 2 * it + 1, 1 - s0, (bk(2), bk(3)), AH, AL)
                pe.wait_ge(qb_copied, 2 * it + 2)
                pe.wait_ge(group_copied, it + 1)
                pe.wait_ge(o_ready, 8 + 4 * it)
                attend(8 * it, SW_UNITS,
                       lambda b, n: QB[:, b, n * P:n * P + P],
                       lambda b, k0, nk: KC[:, k0 * P:(k0 + nk) * P],
                       lambda b, t, x: VC[:, t, 64 * x:64 * x + 64], PL, PT, 8 + 4 * it)
            out_projection(N_SO, N_SO % 2, o_ready, 8)
            layer_sums(2)
            ffn(1, N_F1, N_D1, 24)
            layer_sums(3)

            for m in range(KB):
                pe.wait_ge(h_squared, m + 1)
                pe.matmul(bk(2), con["mean"], SQ[:, m % 2], start=m == 0, stop=m == 7).then_inc(h_summed, 1)
            for m in range(KB):
                pe.wait_ge(m_squared, m + 1)
                pe.matmul(bk(3)[:, 0:MEM], con["mean"], TN[:, m, 0:MEM], start=m == 0, stop=m == 7).then_inc(m_summed, 1)
            s0 = N_MEM % 2
            col_chunk(N_MEM, s0, (bk(4), bk(5)), MH, ML, ready=(m_ready, 0), w=MEM)
            tok_chunk(N_MEM + 1, 1 - s0, [bk(6)[:, 256 * t:256 * t + 256] for t in range(2)], 0, 256, MH, ML)
            pe.wait_ge(n_squared, 1)
            pe.matmul(bk(7).rearrange("p (t c) -> p t c", t=2), con["mean64"], SQH[:, :, 0:MEM], start=True, stop=True).then_inc(n_summed, 1)
            col_chunk(N_FG, N_FG % 2, (bk(1),), AH, AL, ms=(0,), ready=(a_ready, 32))

            def head_norm(i):
                pe.wait_ge(n_squared, i + 1)
                for x in range(2):
                    mm = pe.matmul(bk(4 + x), con["mean64"], SQH[:, x], start=True, stop=True)
                mm.then_inc(n_summed, 1)

            pe.wait_ge(z_abs, 1)
            pe.wait_ge(n_made, 1)
            col_chunk(N_UA, N_UA % 2, (bk(0), bk(1)), AH, AL)
            col_chunk(N_QM, N_QM % 2, (bk(2), bk(3)), AH, AL)
            pe.wait_ge(pu_read, 1)
            col_chunk(N_GA, N_GA % 2, (bk(0), bk(1)), AH, AL, mid=lambda: head_norm(1))
            pe.wait_ge(pool_w_loaded, 16)
            pe.wait_ge(pooled, 1)
            pe.wait_ge(vm_copied, 1)
            for b in range(2):
                mm = pe.matmul(bk(6 + b), WP[:, b], PD[:, b], start=True, stop=True)
            mm.then_inc(pool_mm, 1)
            pe.wait_ge(n_made, 2)
            col_chunk(N_GM, N_GM % 2, (bk(2), bk(3)), AH, AL)

            s0 = N_FX % 2
            with pe.Fori(0, 4) as j:
                pe.wait_ge(n_made, j + 2)
                pe.wait_ge(sg_made, j + 1)
                col_chunk(N_FX + 2 * j, s0, (bk(0), bk(1)), AH, AL)
                pe.wait_ge(fox_v, j)
                pe.wait_ge(sg_made, j + 2)
                tok_chunk(N_FX + 2 * j + 1, 1 - s0, [bk(2)[:, t * P:t * P + P] for t in range(TT)], 0, P, AH, AL, last=False,
                          mid=lambda: head_norm(j + 2))
                col_chunk(N_FX + 2 * j + 1, 1 - s0, (None, bk(3)), AH, AL, ms=(1,))

            pe.wait_ge(n_made, 6)
            pe.wait_ge(fox_v, 4)
            pe.wait_ge(sg_made, 6)
            pe.wait_ge(o_ready, 18)
            attend(U_LAST, LAST_UNITS,
                   lambda b, n: (QKN[:, b, 0] if b < 4 else QMN[:, b - 4])[:, n * P:n * P + P],
                   lambda b, k0, nk: QKN[:, b, 1, 0:nk * P] if b < 4 else KM[:, b - 4],
                   lambda b, t, x: VF[:, b, t, 64 * x:64 * x + 64] if b < 4 else VM[:, t, (b - 4) * P + 64 * x:(b - 4) * P + 64 * x + 64],
                   PL2, PT2[:, :, :, :].rearrange("p s x (k c) -> p s (x k) c", c=P), 18)
            pe.wait_ge(o_ready, 24)
            for j in range(4):
                row_chunk(N_OUT + j, (N_OUT + j) % 2, j, OH, OL, j == 0, j == 3)

        @block.scalar
        def _(act):
            def split_hi(n, slot, uses):
                if not (isinstance(n, int) and n >= N_ALL):
                    if not (isinstance(n, int) and n < 2):
                        act.wait_ge(w_used, n - 1)
                    act.wait_ge(w_loaded[slot], 16 * uses)
                    act.activation(WH[slot][:, :], RAW[slot][:, :], ACT.Copy).then_inc(w_hi, 1)

            def split_next(n):
                split_hi(n + 2, n % 2, (n + 2) // 2 + 1)

            def split_loop(b, step, i):
                split_hi(b + 2 + step * i, b % 2, (b + 2) // 2 + 1 + (step // 2) * i)

            act.preload_act_table_set("natural_log_exp_and_others")
            split_hi(0, 0, 1)
            split_hi(1, 1, 1)
            act.dma_start(PAR[:, :], params).then_inc(consts_in, 16)
            act.dma_start(CON[:, :], consts).then_inc(consts_in, 16)
            act.dma_start(MASK[:, :, :], masks).then_inc(consts_in, 16)
            act.dma_start(SINK[:, :], sinks_bcast).then_inc(consts_in, 16)
            act.dma_start(ROWM[:, :], rel_in[BUCKETS:BUCKETS + SWH, SWH:]).then_inc(consts_in, 16)
            act.dma_start(REL[:, 0:SWH], rel_in[0:BUCKETS, 0:SWH]).then_inc(rel_loaded, 16)
            act.dma_start(REL[:, SWH:], rel_in[0:BUCKETS, SWH:]).then_inc(rel_loaded, 16)
            act.wait_ge(lb_shifted, 1)
            act.activation(LB[:, 2:4], LB[:, 2:4], ACT.Exp).then_inc(lb_exp, 1)
            act.wait_ge(rows_made, 1)
            act.dma_start(bias_rows.rearrange("t h j -> h t j"),
                          ROWS[:, :].unsqueeze(1).broadcast_to([SWH, P, 2 * P])).then_inc(rows_stored, 16)
            act.wait_ge(rows_stored, 16)

            def rstd(out_, in_, scale, eps):
                act.activation(out_, in_, ACT.Ln, bias=eps, scale=scale)
                act.drain()
                return act.activation(out_, out_, ACT.Exp, scale=-0.5)

            def softplus(out_, z, done):
                act.activation(out_, z, ACT.Abs)
                act.drain()
                act.activation(out_, out_, ACT.Exp, scale=-1.0)
                act.drain()
                act.activation(out_, out_, ACT.Ln, bias=con["one"]).then_inc(done, 1)

            def exp_of(ap, done):
                act.activation(ap, ap, ACT.Exp).then_inc(done, 1)

            with act.Fori(0, 4) as it:
                act.preload_act_table_set("natural_log_exp_and_others")
                split_loop(N_HG, 4, it)
                act.wait_ge(o_ready, 2 * it)
                softplus(E1[:, :, :], bank[0][:, :, :], f_soft)
                act.wait_ge(f_logsig, it + 1)
                exp_of(E1[:, :, :], f_sig)
                act.wait_ge(fg_made, it + 1)
                act.activation(EB[:, :, :], E1[:, :, :], ACT.Ln).then_inc(lf_made, 1)
                split_loop(N_HG + 1, 4, it)
                act.drain()
                softplus(E1[:, :, :], bank[1][:, :, :], q_soft)
                act.wait_ge(q_logsig, it + 1)
                exp_of(E1[:, :, :], q_sig)
                act.wait_ge(b_made, it + 1)
                act.activation(EB[:, :, :], BB[:, :, :], ACT.Exp).then_inc(eb_exp, 1)
                act.wait_ge(kd_shifted, it + 1)
                act.activation(KD[:, :, :], KD[:, :, :], ACT.Exp).then_inc(kd_exp, 1)
                for lv in range(LEVELS):
                    act.wait_ge(level_shifted, 7 * it + lv + 1)
                    act.activation(DD[:, lv % 2], DD[:, lv % 2], ACT.Exp).then_inc(level_exp, 1)
                    if lv == 3:
                        split_loop(N_HG + 2, 4, it)
                        act.activation(VV[:, :, :].rearrange("p (a b) c -> p a (b c)", a=2), bank[0][:, :, :], ACT.Copy).then_inc(v_copied, 1)
                split_loop(N_HG + 3, 4, it)
                softplus(E1[:, :, :], bank[1][:, :, :], gate_soft)
                act.wait_ge(gate_logsig, it + 1)
                exp_of(E1[:, :, :], gate_sig)
                act.wait_ge(kd_turned, it + 1)
                act.activation(QT[:, 0, :, 0:3 * P], bank[2][:, :, 0:3 * P], ACT.Copy).then_inc(kd_copied, 1)
                act.wait_ge(o_mm, it + 1)
                act.activation(DD[:, 0], bank[2][:, :, :], ACT.Square).then_inc(o_squared, 1)
                act.drain()
                act.wait_ge(o_summed, it + 1)
                rstd(DD[:, 1], bank[3][:, :, :], float(D // P), con["eps_rms"]).then_inc(o_rstd, 1)

            def layer_norm(idx, g, b, split):
                for m in range(KB):
                    act.wait_ge(y_ready, 8 * idx + m + 1)
                    if m >= 2:
                        act.wait_ge(y_summed, 8 * idx + m - 1)
                    act.activation(SQ[:, m % 2], H[:, m], ACT.Square).then_inc(y_squared, 1)
                act.wait_ge(var_made, idx + 1)
                rstd(VAR[:, :], VAR[:, :], 1.0, con["eps_ln"]).then_inc(rstd_made, 1)
                for m in range(KB):
                    act.wait_ge(normed, 8 * idx + m + 1)
                    ins = act.activation(H[:, m], H[:, m], ACT.Identity, bias=b[:, m:m + 1], scale=g[:, m:m + 1])
                    if split:
                        act.drain()
                        act.activation(AH[:, m], H[:, m], ACT.Copy).then_inc(ah_ready, 1)
                    else:
                        ins.then_inc(h_ready, 1)

            def ffn(n_in, n_down, layer):
                with act.Fori(0, FB // 2) as j:
                    act.preload_act_table_set("silu_and_others")
                    split_loop(n_in, 2, j)
                    act.wait_ge(u_read, FB * layer + 2 * j + 1)
                    act.activation(CB[:, :, :], CA[:, :, :], ACT.Silu).then_inc(a_silu, 1)
                    split_loop(n_in + 1, 2, j)
                split_next(n_down)
                with act.Fori(0, 5) as j:
                    act.preload_act_table_set("natural_log_exp_and_others")
                    split_loop(n_down + 1, 2, j)
                    split_loop(n_down + 2, 2, j)

            act.preload_act_table_set("natural_log_exp_and_others")
            for j in range(4):
                split_next(N_HO + j)
            layer_norm(0, par["mix_g"][:, 0:8], par["mix_b"][:, 0:8], True)
            ffn(N_F0, N_D0, 0)
            act.preload_act_table_set("natural_log_exp_and_others")
            act.dma_start(BIAS[:, :, :], bias_toeplitz).then_inc(bias_loaded, 16)
            layer_norm(1, par["ffn_g"][:, 0:8], par["ffn_b"][:, 0:8], True)

            def attend(u0, units, PL, PT):
                def expo(i):
                    kind, _, tiles = units[i]
                    act.drain()
                    act.wait_ge(l_ready, u0 + i + 1)
                    s = i % 3
                    if kind == "sw":
                        act.activation(SNK[:, s], SNK[:, s], ACT.Exp)
                    rows = rows_of(units[i], PL, s)
                    for r in range(2 * len(tiles)):
                        row = rows[:, r] if kind == "fox" else rows[:, r // 2, r % 2]
                        ins = act.activation(row, row, ACT.Exp, bias=NMAX[:, s, r:r + 1], accum_out=SUMS[:, s, r:r + 1])
                    ins.then_inc(p_exp, 1)

                expo(0)
                for i, (kind, _, tiles) in enumerate(units):
                    if i + 1 < len(units):
                        expo(i + 1)
                    act.wait_ge(p_turned, u0 + i + 1)
                    if i >= 2:
                        act.wait_ge(pv_mm, u0 + i - 1)
                    w = (tiles[0] + 1) * P if kind == "fox" else T
                    act.activation(PT[:, i % 2, :, 0:w], bank[2][:, :, 0:w], ACT.Copy).then_inc(pt_ready, 1)

            split_next(N_KV)
            act.activation(KT[:, :, :], bank[1][:, :, :], ACT.Copy).then_inc(kv_copied, 1)
            split_next(N_KV + 1)
            act.activation(VT[:, :, :].rearrange("p (a b) c -> p a (b c)", a=2), bank[2][:, :, :], ACT.Copy).then_inc(kv_copied, 1)
            with act.Fori(0, 2) as it:
                act.preload_act_table_set("natural_log_exp_and_others")
                for h in range(2):
                    split_loop(N_SQ + h, 2, it)
                    act.activation(QB[:, 2 * h:2 * h + 2], bank[h][:, :, :], ACT.Copy).then_inc(qb_copied, 1)
                attend(8 * it, SW_UNITS, PL, PT[:, :, :, :].rearrange("p s (x k) c -> p s x (k c)", x=2))
            act.preload_act_table_set("natural_log_exp_and_others")
            for j in range(4):
                split_next(N_SO + j)
            layer_norm(2, par["mix_g"][:, 8:16], par["mix_b"][:, 8:16], True)
            ffn(N_F1, N_D1, 1)
            act.preload_act_table_set("natural_log_exp_and_others")
            act.dma_start(MT[:, :, :], mem_t).then_inc(mem_loaded, 16)
            act.dma_start(WP[:, :, :], w_pool).then_inc(pool_w_loaded, 16)
            layer_norm(3, par["ffn_g"][:, 8:16], par["ffn_b"][:, 8:16], False)

            for m in range(KB):
                act.wait_ge(h_ready, m + 1)
                if m >= 2:
                    act.wait_ge(h_summed, m - 1)
                act.activation(SQ[:, m % 2], H[:, m], ACT.Square).then_inc(h_squared, 1)
            act.wait_ge(mem_loaded, 16)
            for m in range(KB):
                act.activation(TN[:, m, 0:MEM], MT[:, m], ACT.Square).then_inc(m_squared, 1)
            act.wait_ge(h_summed, 8)
            act.drain()
            rstd(VAR[:, :], bk(2), 1.0, con["eps_rms"]).then_inc(h_rstd, 1)
            act.wait_ge(m_summed, 8)
            act.drain()
            rstd(MEAN[:, 0:MEM], bk(3)[:, 0:MEM], 1.0, con["eps_rms"]).then_inc(m_rstd, 1)
            for m in range(KB):
                act.wait_ge(tm_made, m + 1)
                act.activation(MH[:, m], MT[:, m], ACT.Copy).then_inc(mh_ready, 1)
            for m in range(KB):
                act.wait_ge(t_made, m + 1)
                act.activation(AH[:, m], TN[:, m], ACT.Copy).then_inc(ah_ready, 1)

            def head_rstd(i, in_, w):
                act.drain()
                act.wait_ge(n_summed, i + 1)
                rstd(RH[:, :, 0:w], in_, 1.0, con["eps_rms"]).then_inc(n_rstd, 1)

            split_next(N_MEM)
            act.activation(SQH[:, :, 0:MEM], bank[2][:, :, 0:MEM], ACT.Square).then_inc(n_squared, 1)
            split_next(N_MEM + 1)
            act.activation(VM[:, :, :], bk(6).rearrange("p (t c) -> p t c", t=2), ACT.Copy).then_inc(vm_copied, 1)
            head_rstd(0, bk(7).rearrange("p (t c) -> p t c", t=2), MEM)
            split_next(N_FG)
            act.wait_ge(z_abs, 1)
            act.activation(FG_[:, 1], FG_[:, 1], ACT.Exp, scale=-1.0)
            act.drain()
            act.activation(FG_[:, 1], FG_[:, 1], ACT.Ln, bias=con["one"][0:8]).then_inc(z_exp, 1)
            act.wait_ge(f_made, 1)
            act.dma_start(forget_rows, FG_[:, 3]).then_inc(f_stored, 16)
            split_next(N_UA)
            act.wait_ge(w_used, N_QM + 1)
            act.activation(SQH[:, :, :], bank[1][:, :, :], ACT.Square).then_inc(n_squared, 1)
            split_next(N_QM)
            head_rstd(1, bank[2][:, :, :], T)
            act.wait_ge(w_used, N_GA + 1)
            act.activation(SG[:, 0:2], bank[0][:, :, :], ACT.Silu).then_inc(sg_made, 1)
            split_next(N_GA)
            act.wait_ge(f_stored, 16)
            act.dma_start(FBC[:, :, :], forget_bcast).then_inc(f_bcast, 16)
            act.wait_ge(w_used, N_GM + 1)
            act.activation(SG[:, 6:8], bank[1][:, :, :], ACT.Silu).then_inc(sg_made, 1)
            split_next(N_GM)

            with act.Fori(0, 4) as j:
                act.preload_act_table_set("natural_log_exp_and_others")
                act.wait_ge(w_used, N_FX + 1 + 2 * j)
                act.activation(SQH[:, :, :], bank[0][:, :, :], ACT.Square).then_inc(n_squared, 1)
                split_loop(N_FX, 2, j)
                head_rstd(j + 2, bank[2][:, :, :], T)
                act.wait_ge(w_used, N_FX + 2 + 2 * j)
                one_j = bass.ds(j, 1)
                act.activation(VF[:, one_j].squeeze(1), bk(2).rearrange("p (t c) -> p t c", t=TT), ACT.Copy).then_inc(fox_v, 1)
                act.activation(SG[:, bass.ds(j + 2, 1)].squeeze(1), bk(3), ACT.Silu).then_inc(sg_made, 1)
                split_loop(N_FX + 1, 2, j)
            act.preload_act_table_set("natural_log_exp_and_others")
            attend(U_LAST, LAST_UNITS, PL2, PT2)
            for j in range(4):
                split_next(N_OUT + j)
            for m in range(KB):
                act.wait_ge(out_ready, m + 1)
                act.dma_start(out[:, m], H[:, m]).then_inc(stored, 16)
            act.wait_ge(stored, 16 * KB)

        @block.vector
        def _(dve):
            def log_sigmoid(ap, z, done):
                dve.scalar_tensor_tensor(ap, z, 0.0, ap, ALU.min, ALU.subtract).then_inc(done, 1)

            for m in range(KB):
                if m % 4 == 0:
                    dve.wait_ge(x_loaded[m // 4], 16)
                dve.tensor_copy(AH[:, m], H[:, m])
                dve.drain()
                dve.tensor_tensor(AL[:, m], H[:, m], AH[:, m].bitcast(F32), ALU.subtract).then_inc(a_ready, 1)
            dve.wait_ge(consts_in, 80)
            lb = par["lb"].rearrange("p (l h) -> p l h", l=2)
            dve.tensor_tensor(LB[:, 0], lb[:, 0], lb[:, 1], ALU.max)
            dve.drain()
            for i in range(2):
                ins = dve.tensor_tensor(LB[:, 2 + i], lb[:, i], LB[:, 0], ALU.subtract)
            ins.then_inc(lb_shifted, 1)
            dve.wait_ge(rel_mm, 1)
            dve.tensor_tensor(ROWS[:, :], bk(7)[0:SWH, 0:2 * P], ROWM[:, :], ALU.add).then_inc(rows_made, 1)
            dve.wait_ge(lb_exp, 1)
            dve.tensor_tensor(LB[:, 1], LB[:, 2], LB[:, 3], ALU.add)
            dve.drain()
            dve.reciprocal(LB[:, 1], LB[:, 1])
            dve.drain()
            dve.tensor_tensor(LB[:, 0], LB[:, 2], LB[:, 1], ALU.mult)
            dve.drain()
            dve.tensor_scalar(LB[:, 1], LB[:, 0], -1.0, 1.0, ALU.mult, ALU.add)
            dve.wait_ge(rows_stored, 16)
            dve.memset(SS[:, :, :, :], 0.0)
            dve.memset(QT[:, :, :, :], 0.0)
            dve.memset(KT_[:, :, :, :], 0.0)
            dve.drain()

            with dve.Fori(0, 4) as it:
                dve.wait_ge(f_soft, it + 1)
                log_sigmoid(E1[:, :, :], bank[0][:, :, :], f_logsig)
                dve.wait_ge(f_sig, it + 1)
                for h in range(2):
                    col = bass.ds(2 * it + h, 1)
                    dve.tensor_scalar(E1[:, h], E1[:, h], LB[:, 1, col], LB[:, 0, col], ALU.mult, ALU.add)
                dve.drain()
                dve.tensor_scalar(KK[:, :, :], E1[:, :, :], -1.0, 1.0, ALU.mult, ALU.add)
                dve.drain()
                dve.tensor_scalar(E1[:, :, :], E1[:, :, :], TINY, None, ALU.max).then_inc(fg_made, 1)
                dve.wait_ge(lf_made, it + 1)
                for h in range(2):
                    ins = dve.tensor_tensor_scan(BB[:, h], con["carry"], EB[:, h], 0.0, ALU.mult, ALU.add)
                ins.then_inc(b_made, 1)
                dve.wait_ge(b_made, it + 1)
                dve.wait_ge(q_soft, it + 1)
                log_sigmoid(E1[:, :, :], bank[1][:, :, :], q_logsig)
                dve.wait_ge(q_sig, it + 1)
                dve.tensor_tensor(QQ[:, :, :], bank[1][:, :, :], E1[:, :, :], ALU.mult).then_inc(q_read, 1)
                B4 = BB[:, :, :].rearrange("p h (c t) -> p (h c) t", t=P)
                dve.tensor_tensor(KD[:, :, :].rearrange("p h (c t) -> p (h c) t", t=P),
                                  B4[:, :, P - 1:P].broadcast_to([P, 8, P]), B4, ALU.subtract).then_inc(kd_shifted, 1)

                def shift(lv):
                    m = 64 >> lv
                    b4, d4 = halves(BB[:, :, :], m), halves(DD[:, lv % 2], m)
                    mid = b4[:, :, 0, m - 1:m].broadcast_to([P, 2 * T // (2 * m), m])
                    dve.tensor_tensor(d4[:, :, 1], b4[:, :, 1], mid, ALU.subtract)
                    dve.tensor_tensor(d4[:, :, 0], mid, b4[:, :, 0], ALU.subtract).then_inc(level_shifted, 1)

                def scale_qk(lv):
                    m = 64 >> lv
                    dve.wait_ge(level_exp, 7 * it + lv + 1)
                    d4 = halves(DD[:, lv % 2], m)
                    dve.tensor_tensor(halves(QT[:, lv % 2], m)[:, :, 1], halves(QQ[:, :, :], m)[:, :, 1], d4[:, :, 1], ALU.mult)
                    dve.tensor_tensor(halves(KT_[:, lv % 2], m)[:, :, 0], halves(KK[:, :, :], m)[:, :, 0], d4[:, :, 0],
                                      ALU.mult).then_inc(level_made, 1)

                def pick(lv):
                    dve.wait_ge(level_mm, 8 * it + lv + 1)
                    dve.memset(PAD[:, :], 0.0)
                    for h in range(2):
                        ins = dve.copy_predicated(SS[:, h], MASK[:, lv:lv + 1].bitcast(U32).broadcast_to([P, TT, P]),
                                                  bk(4 + 2 * (lv % 2) + h).rearrange("p (c t) -> p c t", t=P))
                    ins.then_inc(level_picked, 1)

                for st in range(LEVELS + 4):
                    dve.drain()
                    if st < LEVELS:
                        shift(st)
                    if st == 0:
                        dve.wait_ge(eb_exp, it + 1)
                        dve.tensor_tensor(QI[:, :, :], QQ[:, :, :], EB[:, :, :], ALU.mult)
                    if st == 1:
                        dve.wait_ge(kd_exp, it + 1)
                        dve.tensor_tensor(KD[:, :, :], KD[:, :, :], KK[:, :, :], ALU.mult).then_inc(kd_made, 1)
                    if 3 <= st:
                        pick(st - 3)
                    if 1 <= st <= LEVELS:
                        scale_qk(st - 1)
                dve.wait_ge(gate_soft, it + 1)
                log_sigmoid(E1[:, :, :], bank[1][:, :, :], gate_logsig)
                dve.wait_ge(gate_sig, it + 1)
                dve.tensor_tensor(E1[:, :, :], E1[:, :, :], bank[1][:, :, :], ALU.mult).then_inc(gate_read, 1)
                dve.drain()
                dve.wait_ge(kv_mm, it + 1)
                dve.tensor_copy(BB[:, :, 0:P], bank[3][:, :, 0:P])
                for c in range(1, TT - 1):
                    dve.drain()
                    for h in range(2):
                        ins = dve.scalar_tensor_tensor(BB[:, h, c * P:c * P + P], BB[:, h, (c - 1) * P:c * P],
                                                       EB[:, h, c * P + P - 1:c * P + P], bk(6 + h)[:, c * P:c * P + P],
                                                       ALU.mult, ALU.add)
                ins.then_inc(state_made, 1)
                dve.wait_ge(o_rstd, it + 1)
                dve.tensor_tensor(KK[:, :, :], bank[2][:, :, :], DD[:, 1], ALU.mult)
                dve.drain()
                dve.scalar_tensor_tensor(KK[:, :, :], KK[:, :, :], par["gnorm"], E1[:, :, :], ALU.mult, ALU.mult)
                dve.drain()
                for h in range(2):
                    dve.tensor_copy(OH[:, bass.ds(2 * it + h, 1)].squeeze(1), KK[:, h])
                dve.drain()
                for h in range(2):
                    col = bass.ds(2 * it + h, 1)
                    dve.tensor_tensor(OL[:, col].squeeze(1), KK[:, h], OH[:, col].squeeze(1).bitcast(F32), ALU.subtract).then_inc(o_ready, 1)
                dve.drain()

            def layer_norm(idx, n_last, split):
                for m in range(KB):
                    if m < 7:
                        dve.wait_ge(r_done, 7 * idx + m + 1)
                    else:
                        dve.wait_ge(w_used, n_last + 1)
                    dve.scalar_tensor_tensor(H[:, m], H[:, m], ALPHA, bk(m), ALU.mult, ALU.add).then_inc(y_ready, 1)
                dve.wait_ge(y_summed, 8 * idx + 8)
                dve.drain()
                dve.tensor_copy(MEAN[:, :], bk(0))
                dve.drain()
                dve.tensor_tensor(VAR[:, :], MEAN[:, :], MEAN[:, :], ALU.mult)
                dve.drain()
                dve.tensor_tensor(VAR[:, :], bk(1), VAR[:, :], ALU.subtract)
                dve.drain()
                dve.tensor_scalar(VAR[:, :], VAR[:, :], 0.0, None, ALU.max).then_inc(var_made, 1)

                def centre(m):
                    dve.tensor_tensor(H[:, m], H[:, m], MEAN[:, :], ALU.subtract)

                def low(m):
                    dve.wait_ge(ah_ready, 8 * idx + m + 1)
                    dve.tensor_tensor(AL[:, m], H[:, m], AH[:, m].bitcast(F32), ALU.subtract).then_inc(a_ready, 1)

                centre(0)
                centre(1)
                dve.wait_ge(rstd_made, idx + 1)
                for m in range(KB):
                    dve.drain()
                    dve.tensor_tensor(H[:, m], H[:, m], VAR[:, :], ALU.mult).then_inc(normed, 1)
                    if m + 2 < KB:
                        centre(m + 2)
                    if split and m >= 2:
                        low(m - 2)
                if split:
                    low(6)
                    low(7)

            def ffn(layer, n_in):
                def conv(out_, src, ab, j):
                    for c in range(2):
                        blk = bass.ds(2 * j + c, 1)
                        tap = [CONVW[:, layer, t, ab, blk] for t in range(3)]
                        dve.tensor_scalar(out_[:, c], src[:, c], tap[2], CONVB[:, layer, ab, blk], ALU.mult, ALU.add)
                    for d in (1, 2):
                        dve.drain()
                        for c in range(2):
                            blk = bass.ds(2 * j + c, 1)
                            ins = dve.scalar_tensor_tensor(out_[:, c, d:T], src[:, c, 0:T - d], CONVW[:, layer, 2 - d, ab, blk],
                                                           out_[:, c, d:T], ALU.mult, ALU.add)
                    return ins

                with dve.Fori(0, FB // 2) as j:
                    dve.drain()
                    dve.wait_ge(w_used, n_in + 1 + 2 * j)
                    conv(CA, bank[0], 0, j).then_inc(u_read, 1)
                    dve.drain()
                    dve.wait_ge(a_silu, 11 * layer + j + 1)
                    dve.wait_ge(w_used, n_in + 2 + 2 * j)
                    conv(CA, bank[1], 1, j).then_inc(u_read, 1)
                    dve.drain()
                    dve.tensor_tensor(CA[:, :, :], CA[:, :, :], CB[:, :, :], ALU.mult)
                    dve.drain()
                    pair = bass.ds(2 * j, 2)
                    dve.tensor_copy(GH[:, pair], CA[:, :, :])
                    dve.drain()
                    dve.tensor_tensor(GL[:, pair], CA[:, :, :], GH[:, pair].bitcast(F32), ALU.subtract).then_inc(g_ready, 1)

            layer_norm(0, N_HO + 3, True)
            ffn(0, N_F0)
            layer_norm(1, N_D0 + 10, True)

            def attend(u0, units, PL, first_stage, finish, sink):
                def logits(i):
                    u, s = units[i], i % 3
                    rows, nmax = rows_of(u, PL, s), per_row(u, NMAX, s)
                    dve.drain()
                    dve.wait_ge(s_mm, u0 + i + 1)
                    if i >= 3:
                        dve.wait_ge(p_turned, u0 + i - 2)
                    if u[0] == "fox":
                        first_stage(u, bank[i % 2][:, :, 0:(u[2][0] + 1) * P], rows)
                    else:
                        first_stage(u, bank[i % 2][:, :, :].rearrange("p x (t s) -> p x t s", t=2), rows)
                    dve.drain()
                    ins = dve.tensor_reduce(nmax, rows, AX_X, ALU.max, negate=True)
                    if sink is not None:
                        dve.drain()
                        of_rows = sink(u[1]).unsqueeze(2).broadcast_to([P, 2, 2])
                        dve.scalar_tensor_tensor(nmax, of_rows, -1.0, nmax, ALU.mult, ALU.min)
                        dve.drain()
                        ins = dve.tensor_tensor(per_row(u, SNK, s), of_rows, nmax, ALU.add)
                    ins.then_inc(l_ready, 1)

                def end_pair(i):
                    if ends_pair(units, i):
                        dve.drain()
                        dve.wait_ge(pv_mm, u0 + i + 1)
                        finish(units[i][1])

                logits(0)
                for i, u in enumerate(units):
                    s, n_rows = i % 3, 2 * len(u[2])
                    if i + 1 < len(units):
                        logits(i + 1)
                    end_pair(i - 2)
                    dve.wait_ge(p_exp, u0 + i + 1)
                    if sink is not None:
                        dve.tensor_tensor(SUMS[:, s], SUMS[:, s], SNK[:, s], ALU.add)
                        dve.drain()
                    dve.reciprocal(RDEN[:, s, 0:n_rows], SUMS[:, s, 0:n_rows])
                    dve.drain()
                    rows = rows_of(u, PL, s)
                    for r in range(n_rows):
                        row = rows[:, r] if u[0] == "fox" else rows[:, r // 2, r % 2]
                        ins = dve.tensor_scalar(row, row, RDEN[:, s, r:r + 1], None, ALU.mult)
                    ins.then_inc(p_ready, 1)
                end_pair(len(units) - 2)
                end_pair(len(units) - 1)

            dve.wait_ge(kv_copied, 2)
            dve.wait_ge(bias_loaded, 16)
            SINK3 = SINK[:, :].rearrange("p (o x b) -> p o x b", o=2, x=2)
            BIAS5 = BIAS[:, :, :].rearrange("p (o x b) s -> p o x b s", o=2, x=2)
            with dve.Fori(0, 2) as it:
                one_it = bass.ds(it, 1)
                dve.tensor_copy(KC[:, :], KT[:, one_it].squeeze(1))
                dve.tensor_copy(VC[:, :, :], VT[:, :, bass.ds(it * P, P)]).then_inc(group_copied, 1)

                def sw_logits(u, src, dst):
                    bias = BIAS5[:, one_it, :, u[1]].squeeze(1)
                    first = u[2][0] == 0
                    if first:
                        dve.memset(dst[:, :, 0, 0:P], NEG)
                    for t in range(2):
                        lo = P if first and t == 0 else 0
                        dve.scalar_tensor_tensor(dst[:, :, t, lo:], src[:, :, t, lo:], SCALE, bias[:, :, lo:], ALU.mult, ALU.add)

                def sw_finish(b):
                    o = bk(6 + b % 2)
                    col = bass.ds(4 * it + b, 1)
                    dve.tensor_copy(OH[:, col].squeeze(1), o)
                    dve.drain()
                    dve.tensor_tensor(OL[:, col].squeeze(1), o, OH[:, col].squeeze(1).bitcast(F32), ALU.subtract).then_inc(o_ready, 1)

                attend(8 * it, SW_UNITS, PL, sw_logits, sw_finish, lambda b: SINK3[:, one_it, :, b].squeeze(1))
            layer_norm(2, N_SO + 3, True)
            ffn(1, N_F1)
            layer_norm(3, N_D1 + 10, False)

            dve.wait_ge(m_rstd, 1)
            for m in range(KB):
                dve.scalar_tensor_tensor(MT[:, m], MT[:, m], par["mem_g"][:, m:m + 1], MEAN[:, 0:MEM],
                                         ALU.mult, ALU.mult).then_inc(tm_made, 1)
            for m in range(KB):
                dve.wait_ge(mh_ready, m + 1)
                dve.tensor_tensor(ML[:, m], MT[:, m], MH[:, m].bitcast(F32), ALU.subtract).then_inc(m_ready, 1)
            dve.wait_ge(h_rstd, 1)
            for m in range(KB + 2):
                if m < KB:
                    dve.scalar_tensor_tensor(TN[:, m], H[:, m], par["norm_g"][:, m:m + 1], VAR[:, :],
                                             ALU.mult, ALU.mult).then_inc(t_made, 1)
                if m >= 2:
                    dve.wait_ge(ah_ready, 24 + m - 1)
                    dve.tensor_tensor(AL[:, m - 2], TN[:, m - 2], AH[:, m - 2].bitcast(F32), ALU.subtract).then_inc(a_ready, 1)

            def head_norm(i, src, gains, out_, w):
                dve.wait_ge(n_rstd, i + 1)
                for x in range(2):
                    ins = dve.scalar_tensor_tensor(out_[:, x, 0:w], src[:, x, 0:w], gains[x], RH[:, x, 0:w], ALU.mult, ALU.mult)
                ins.then_inc(n_made, 1)

            head_norm(0, bank[2], (par["mem_kg"], par["mem_kg"]), KM, MEM)
            dve.wait_ge(w_used, N_FG + 1)
            dve.tensor_scalar(FG_[:, 0], bk(1)[0:8], par["forget_b"][0:8], None, ALU.add)
            dve.drain()
            dve.scalar_tensor_tensor(FG_[:, 1], FG_[:, 0], -1.0, FG_[:, 0], ALU.mult, ALU.max).then_inc(z_abs, 1)
            dve.tensor_scalar(FG_[:, 2], FG_[:, 0], 0.0, None, ALU.min)
            dve.wait_ge(z_exp, 1)
            dve.drain()
            dve.tensor_tensor(FG_[:, 2], FG_[:, 2], FG_[:, 1], ALU.subtract)
            dve.drain()
            dve.tensor_tensor_scan(FG_[:, 3], con["one"][0:8].broadcast_to([8, T]), FG_[:, 2], 0.0, ALU.mult, ALU.add).then_inc(f_made, 1)

            dve.wait_ge(w_used, N_UA + 1)
            dve.tensor_copy(PU[:, :, :], bank[0][:, :, :]).then_inc(pu_read, 1)
            dve.drain()

            def widen(dst, src, b, lo, d):
                dve.tensor_copy(dst[lo:P, b, 0:d], src[lo:P, b, 0:d])
                dve.tensor_tensor(dst[lo:P, b, d:T], src[lo:P, b, d:T], src[lo:P, b, 0:T - d], ALU.add)

            widen(PS, PU, 0, 0, 1)
            widen(PS, PU, 1, 0, 1)
            dve.drain()
            dve.tensor_copy(PD[0:64, 0], PS[0:64, 0])
            widen(PD, PS, 0, 64, 2)
            widen(PD, PS, 1, 0, 2)
            dve.drain()
            widen(PS, PD, 1, 0, 4)
            dve.drain()
            dve.tensor_copy(PD[0:64, 1], PS[0:64, 1])
            widen(PD, PS, 1, 64, 8)
            dve.drain()
            inv = con["inv_count"].rearrange("p (b t) -> p b t", b=2)
            dve.tensor_tensor(PD[:, :, :], PD[:, :, :], inv, ALU.mult)
            dve.drain()
            dve.tensor_tensor(PD[:, :, :], PD[:, :, :], PU[:, :, :], ALU.subtract).then_inc(pooled, 1)
            head_norm(1, bank[1], (par["mem_qg"], par["mem_qg"]), QMN, T)
            dve.wait_ge(pool_mm, 1)
            dve.wait_ge(sg_made, 1)
            for b in range(2):
                dve.scalar_tensor_tensor(TP[:, :], bk(6 + b), par["pool_scale"][:, b:b + 1], SG[:, b], ALU.mult, ALU.mult)
                dve.drain()
                dve.tensor_copy(OH[:, b], TP[:, :])
                dve.drain()
                dve.tensor_tensor(OL[:, b], TP[:, :], OH[:, b].bitcast(F32), ALU.subtract).then_inc(o_ready, 1)
                dve.drain()

            with dve.Fori(0, 4) as j:
                head_norm(j + 2, bank[0], (par["fox_qg"], par["fox_kg"]), QKN[:, bass.ds(j, 1)].squeeze(1), T)

            def last_logits(u, src, dst):
                kind, b, tiles = u
                if kind == "mem":
                    dve.tensor_scalar(dst, src, SCALE, None, ALU.mult)
                    return
                w = (tiles[0] + 1) * P
                dve.scalar_tensor_tensor(dst, src, SCALE, FBC[:, 2 * b:2 * b + 2, 0:w], ALU.mult, ALU.subtract)
                dve.drain()
                diag = dst[:, :, w - P:w]
                dve.tensor_tensor(diag, diag, con["causal"].unsqueeze(1).broadcast_to([P, 2, P]), ALU.add)

            def gated(b):
                dve.tensor_tensor(TO[:, :], bk(6 + b % 2), SG[:, 2 + b], ALU.mult)
                dve.drain()
                dve.tensor_copy(OH[:, 2 + b], TO[:, :])
                dve.drain()
                dve.tensor_tensor(OL[:, 2 + b], TO[:, :], OH[:, 2 + b].bitcast(F32), ALU.subtract).then_inc(o_ready, 1)

            dve.wait_ge(f_bcast, 16)
            dve.wait_ge(sg_made, 6)
            attend(U_LAST, LAST_UNITS, PL2, last_logits, gated, None)
            dve.drain()
            for m in range(KB):
                if m < 7:
                    dve.wait_ge(r_done, 28 + m + 1)
                else:
                    dve.wait_ge(w_used, N_ALL)
                dve.tensor_tensor(H[:, m], H[:, m], bk(m), ALU.add).then_inc(out_ready, 1)


def col_chunks(w, cols):
    out = []
    for parts in cols:
        c = np.concatenate([w[:, a:b] for a, b in parts], axis=1)
        if c.shape[1] < 256:
            c = np.concatenate([c, np.zeros((c.shape[0], 256 - c.shape[1]), c.dtype)], axis=1)
        out.append(c.reshape(8, P, 256).transpose(1, 0, 2).reshape(1, P, 2048))
    return out


def row_chunks(w):
    n = w.shape[0] // 256
    return [w.reshape(n, 2, P, 1024).transpose(0, 2, 1, 3).reshape(n, P, 2048)]


def per_feature(a):
    n = a.shape[-1] // P
    return np.moveaxis(a.reshape(*a.shape[:-1], n, P), -1, 0).reshape(P, -1)


def constants():
    c = np.zeros((P, NCON), np.float32)
    i = np.arange(P)

    def put(name, v):
        a, b = CCOL[name]
        c[:, a:b] = v

    put("ident", np.eye(P))
    put("mean", 1.0 / D)
    put("mean64", (i[:, None] // 64 == i[None, :] // 64) / 64.0)
    put("causal", np.where(i[None, :] <= i[:, None], 0.0, NEG))
    put("carry", (np.arange(T) % P != 0).astype(np.float32)[None])
    put("eps_ln", LN_EPS)
    put("eps_rms", RMS_EPS)
    put("one", 1.0)
    win = np.array(POOL_WINDOWS)[(i[:, None] // 64) + 2 * np.arange(2)[None]]
    put("inv_count", (1.0 / np.minimum(np.arange(T)[None, None] + 1, win[:, :, None])).reshape(P, -1))
    masks = np.zeros((P, 8, P), np.float32)
    s, t = i[:, None], i[None, :]
    for lv in range(LEVELS):
        m = 64 >> lv
        masks[:, lv] = (s // (2 * m) == t // (2 * m)) & (s % (2 * m) < m) & (t % (2 * m) >= m)
    masks[:, 7] = s == t
    j = np.arange(2 * P)
    dist = P - j
    ok = (dist >= 0) & (dist < P)
    dc = np.clip(dist, 0, P - 1)
    d = np.maximum(dc, 1).astype(np.float32)
    log_b = 16 + (np.log(d / np.float32(16)) / np.float32(np.log(8.0)) * 16).astype(np.int32)
    bucket = np.where(dc < 16, dc, np.minimum(log_b, BUCKETS - 1))
    hot = ((bucket[None] == np.arange(BUCKETS)[:, None]) & ok[None]).astype(np.float32)
    return c, masks, hot, np.where(ok, 0.0, NEG).astype(np.float32)


def kernel(**inputs):
    import concourse.bacc as bacc
    from concourse.bass_utils import run_bass_kernel_spmd

    a = {k: np.asarray(v) for k, v in inputs.items()}
    con, masks, hot, row_mask = constants()
    parts = []
    w = a["hgrn_w_in"][0]
    for hp in range(4):
        for base in (1024, 0, 2048, 3072):
            parts += col_chunks(w, [[(base + 256 * hp, base + 256 * hp + 256)]])
    parts += row_chunks(a["hgrn_w_out"][0])
    ffn_in = [[[(256 * j, 256 * j + 256)], [(FFN + 256 * j, FFN + 256 * j + 256)]] for j in range(FB // 2)]
    heads = [8 * o + b + 4 * x for o in range(2) for b in range(4) for x in range(2)]
    for layer in range(2):
        if layer == 1:
            parts += col_chunks(a["shared_w_kv"], [[(0, 256)], [(256, 512)]])
            parts += col_chunks(a["swa_w_q"][0], [[(64 * h, 64 * h + 64) for h in heads[4 * c:4 * c + 4]] for c in range(4)])
            wo = a["swa_w_out"][0]
            parts += row_chunks(np.concatenate([wo[64 * h:64 * h + 64] for h in heads], axis=0))
        for pair in ffn_in:
            parts += col_chunks(a["ffn_w_in"][layer], pair)
        parts += row_chunks(a["ffn_w_out"][layer])
    parts += col_chunks(a["w_mem_kv_2"][0], [[(0, 256)], [(256, 512)]])
    w = a["w_in_2"][0]
    ua, ga, qb, kb, vb, fb, gb, qm, gm = np.cumsum([0, 256, 256, 512, 512, 512, 8, 512, 256])
    parts += col_chunks(w, [[(fb, fb + 8)]])
    parts += col_chunks(w, [[(c, c + 256)] for c in (ua, qm, ga, gm)])
    for j in range(4):
        parts += col_chunks(w, [[(qb + P * j, qb + P * j + P), (kb + P * j, kb + P * j + P)],
                                [(vb + P * j, vb + P * j + P), (gb + P * j, gb + P * j + P)]])
    parts += row_chunks(a["w_out_2"][0])
    stream = np.concatenate(parts, axis=0)

    def twice(v):
        return np.concatenate([v, v]).reshape(P, 1)

    vec = {
        "lb": per_feature(a["hgrn_lb_logits"]), "gnorm": a["hgrn_gnorm_w"].reshape(P, 1),
        "conv_w": per_feature(a["ffn_conv_w"]), "conv_b": per_feature(a["ffn_conv_b"]),
        "mix_g": per_feature(a["ln_mix_g"]), "mix_b": per_feature(a["ln_mix_b"]),
        "ffn_g": per_feature(a["ln_ffn_g"]), "ffn_b": per_feature(a["ln_ffn_b"]),
        "norm_g": per_feature(a["norm_g_2"]), "mem_g": per_feature(a["mem_norm_g_2"]),
        "pool_scale": per_feature(a["pool_scale_2"]),
        "fox_qg": twice(a["fox_q_g_2"][0]), "fox_kg": twice(a["fox_k_g_2"][0]),
        "mem_qg": twice(a["mem_q_g_2"][0]), "mem_kg": twice(a["mem_k_g_2"][0]),
        "forget_b": np.concatenate([a["b_f_2"][0], np.zeros(P - 8, np.float32)]).reshape(P, 1),
    }
    params = np.concatenate([vec[n] for n, _ in PARAMS], axis=1)
    rel_in = np.zeros((BUCKETS + SWH, SWH + 2 * P), np.float32)
    rel_in[0:BUCKETS, 0:SWH] = a["rel_bias"]
    rel_in[0:BUCKETS, SWH:] = hot
    rel_in[BUCKETS:, SWH:] = row_mask
    w_pool = np.zeros((P, 2, P), np.float32)
    for g in range(4):
        r = 64 * (g % 2)
        w_pool[r:r + 64, g // 2, r:r + 64] = a["w_pool_2"][0, g]
    arrays = {
        "stream": stream,
        "x_t": a["x"][0].reshape(T, KB, P).transpose(2, 1, 0),
        "mem_t": a["mem_2"][0].reshape(MEM, KB, P).transpose(2, 1, 0),
        "params": params, "consts": con, "masks": masks, "sinks": a["swa_sinks"].reshape(SWH),
        "rel_in": rel_in, "w_pool": w_pool,
    }
    arrays = {k: np.ascontiguousarray(v) for k, v in arrays.items()}
    nc = bacc.Bacc("TRN2", target_bir_lowering=False, num_devices=1)
    args = [nc.dram_tensor(k, v.shape, mybir.dt.from_np(v.dtype), kind="ExternalInput").ap() for k, v in arrays.items()]
    out = nc.dram_tensor("out", (P, KB, T), F32, kind="ExternalOutput").ap()
    build(nc, *args, out)
    r = run_bass_kernel_spmd(nc, [arrays], core_ids=[0])
    got = r.results[0]["out"]
    return np.ascontiguousarray(got.transpose(2, 1, 0)).reshape(1, T, D)
```

```python
from contextlib import ExitStack

import numpy as np

import concourse.bass as bass
from concourse import mybir

F32 = mybir.dt.float32
F32R = mybir.dt.float32r
U32 = mybir.dt.uint32
ALU = mybir.AluOpType
ACT = mybir.ActivationFunctionType
AX_X = mybir.AxisListType.X

P = 128
D = 1024
KB = D // P
T = 512
TT = T // P
FFN = 2816
FB = FFN // P
DEPTH = 2
HEADS = 8
LEVELS = 7
SWH = 16
MEM = 256
ALPHA = (2.0 * DEPTH) ** 0.25
LN_EPS = 1e-5
RMS_EPS = 1e-6
NEG = -1e30
TINY = 2.0 ** -64
SCALE = 64 ** -0.5
BUCKETS = 32
POOL_WINDOWS = (2, 4, 8, 16)

N_HG = 0
N_HO = N_HG + 16
N_F0 = N_HO + 4
N_D0 = N_F0 + FB
N_KV = N_D0 + FB // 2
N_SQ = N_KV + 2
N_SO = N_SQ + 4
N_F1 = N_SO + 4
N_D1 = N_F1 + FB
N_MEM = N_D1 + FB // 2
N_FG = N_MEM + 2
N_UA = N_FG + 1
N_QM = N_UA + 1
N_GA = N_QM + 1
N_GM = N_GA + 1
N_FX = N_GM + 1
N_OUT = N_FX + 8
N_ALL = N_OUT + 4

PARAMS = [("lb", 16), ("gnorm", 1), ("conv_w", 264), ("conv_b", 88), ("mix_g", 16), ("mix_b", 16),
          ("ffn_g", 16), ("ffn_b", 16), ("norm_g", 8), ("mem_g", 8), ("pool_scale", 2),
          ("fox_qg", 1), ("fox_kg", 1), ("mem_qg", 1), ("mem_kg", 1), ("forget_b", 1)]
CONSTS = [("ident", P), ("mean", P), ("mean64", P), ("causal", P), ("carry", T), ("eps_ln", 1),
          ("eps_rms", 1), ("one", 1), ("inv_count", 2 * T)]


def columns(table):
    at, out = 0, {}
    for name, n in table:
        out[name] = (at, at + n)
        at += n
    return out, at


PCOL, NPAR = columns(PARAMS)
CCOL, NCON = columns(CONSTS)


def build(nc, stream, x_t, mem_t, params, consts, masks, sinks, rel_in, w_pool, out):
    bias_rows = nc.dram_tensor("bias_rows", (P, SWH, 2 * P), F32).ap()
    forget_rows = nc.dram_tensor("forget_rows", (8, T), F32).ap()
    bias_toeplitz = bass.AP(bias_rows.tensor, 0, [[SWH * 2 * P - 1, P], [2 * P, SWH], [1, 2 * P]])
    forget_bcast = bass.AP(forget_rows.tensor, 0, [[0, P], [T, 8], [1, T]])
    sinks_bcast = bass.AP(sinks.tensor, 0, [[0, P], [1, SWH]])

    with ExitStack() as ctx:
        def sb(name, shape, dt=F32, scope=ctx):
            return scope.enter_context(nc.sbuf_tensor(name, shape, dt))

        def sem(name):
            return ctx.enter_context(nc.semaphore(name))

        H = sb("H", [P, KB, T])
        with ExitStack() as s:
            PL2 = sb("PL2", [P, 3, 2, T], F32, s)
            PT2 = sb("PT2", [P, 2, 2, T], F32, s)
            TO = sb("TO", [P, T], F32, s)
        AH = sb("AH", [P, KB, T], F32R)
        AL = sb("AL", [P, KB, T], F32R)
        RAW = [sb(f"RAW{s}", [P, 2048]) for s in range(2)]
        WH = [sb(f"WH{s}", [P, 2048], F32R) for s in range(2)]
        WL = [sb(f"WL{s}", [P, 2048], F32R) for s in range(2)]
        PAR = sb("PAR", [P, NPAR])
        CON = sb("CON", [P, NCON])
        MASK = sb("MASK", [P, 8, P])
        SINK = sb("SINK", [P, SWH])
        LB = sb("LB", [P, 4, 8])
        SMALL = sb("SMALL", [P, 4, 3, 4])
        PAD = sb("PAD", [P, 1])
        par = {k: PAR[:, a:b] for k, (a, b) in PCOL.items()}
        con = {k: CON[:, a:b] for k, (a, b) in CCOL.items()}
        CONVW = par["conv_w"].rearrange("p (l t a j) -> p l t a j", l=2, t=3, a=2)
        CONVB = par["conv_b"].rearrange("p (l a j) -> p l a j", l=2, a=2)
        NMAX, SUMS, SNK, RDEN = (SMALL[:, i] for i in range(4))

        with ExitStack() as s:
            sb("OH_HEAD", [P, 2, T], F32, s)
            SQH = sb("SQH", [P, 2, T], F32, s)
            RH = sb("RH", [P, 2, T], F32, s)
            PU = sb("PU", [P, 2, T], F32, s)
            sb("OL_HEAD", [P, 2, T], F32, s)
            PS = sb("PS", [P, 2, T], F32, s)
            PD = sb("PD", [P, 2, T], F32, s)
            TP = sb("TP", [P, T], F32, s)
            WP = sb("WP", [P, 2, P], F32, s)
        with ExitStack() as s:
            OH = sb("OH", [P, KB, T], F32R, s)
            OL = sb("OL", [P, KB, T], F32R, s)
            with ExitStack() as s1:
                one = lambda name: sb(name, [P, 2, T], F32, s1)
                E1, E2, KK, BB, EB, QQ, QI, KD = (one(n) for n in ("E1", "E2", "KK", "BB", "EB", "QQ", "QI", "KD"))
                DD = sb("DD", [P, 2, 2, T], F32, s1)
                QT = sb("QT", [P, 2, 2, T], F32, s1)
                KT_ = sb("KT_", [P, 2, 2, T], F32, s1)
                SS = sb("SS", [P, 2, TT, P], F32, s1)
                VV = sb("VV", [P, TT, 2 * P], F32, s1)
            with ExitStack() as s1:
                REL = sb("REL", [BUCKETS, SWH + 2 * P], F32, s1)
                ROWS = sb("ROWS", [SWH, 2 * P], F32, s1)
                ROWM = sb("ROWM", [SWH, 2 * P], F32, s1)
            with ExitStack() as s1:
                BIAS = sb("BIAS", [P, SWH, 2 * P], F32, s1)
                KT = sb("KT", [P, 2, T], F32, s1)
                VT = sb("VT", [P, TT, 2 * P], F32, s1)
                KC = sb("KC", [P, T], F32, s1)
                VC = sb("VC", [P, TT, P], F32, s1)
                QB = sb("QB", [P, 4, T], F32, s1)
                PL = sb("PL", [P, 3, 4, 2 * P], F32, s1)
                PT = sb("PT", [P, 2, 8, P], F32, s1)
            with ExitStack() as s1:
                MT = sb("MT", [P, KB, MEM], F32, s1)
                MH = sb("MH", [P, KB, MEM], F32R, s1)
                ML = sb("ML", [P, KB, MEM], F32R, s1)
                TN = sb("TN", [P, KB, T], F32, s1)
            with ExitStack() as s1:
                FBC = sb("FBC", [P, 8, T], F32, s1)
                KM = sb("KM", [P, 2, MEM], F32, s1)
                VM = sb("VM", [P, 2, MEM], F32, s1)
                QKN = sb("QKN", [P, 4, 2, T], F32, s1)
                VF = sb("VF", [P, 4, TT, P], F32, s1)
                SG = sb("SG", [P, KB, T], F32, s1)
                QMN = sb("QMN", [P, 2, T], F32, s1)
                FG_ = SG[0:8, 2:6]
        with ExitStack() as s:
            GH = sb("GH", [P, FB, T], F32R, s)
            GL = sb("GL", [P, FB, T], F32R, s)
            with ExitStack() as s1:
                CA = sb("CA", [P, 2, T], F32, s1)
                CB = sb("CB", [P, 2, T], F32, s1)
            with ExitStack() as s1:
                MEAN = sb("MEAN", [P, T], F32, s1)
                VAR = sb("VAR", [P, T], F32, s1)

        with ExitStack() as s:
            sb("BEHIND", [P, 48 * 256], F32, s)
            SQ = sb("SQ", [P, 4, T], F32, s)
            SY = sb("SY", [P, T], F32, s)
            SY2 = sb("SY2", [P, T], F32, s)

        bank = [ctx.enter_context(nc.psum_tensor(f"pair{i}", [P, 2, T], F32)) for i in range(4)]

        def bk(i):
            return bank[i // 2][:, i % 2]

        w_loaded = [sem("w_loaded0"), sem("w_loaded1")]
        w_hi, w_lo, w_used = sem("w_hi"), sem("w_lo"), sem("w_used")
        consts_in, rel_loaded, mem_loaded = sem("consts_in"), sem("rel_loaded"), sem("mem_loaded")
        x_loaded = [sem("x_loaded0"), sem("x_loaded1")]
        a_ready, ah_ready, o_ready, g_ready = sem("a_ready"), sem("ah_ready"), sem("o_ready"), sem("g_ready")
        m_ready, mh_ready = sem("m_ready"), sem("mh_ready")
        rel_mm, rows_made, rows_stored, bias_loaded = (sem(n) for n in ("rel_mm", "rows_made", "rows_stored", "bias_loaded"))
        lb_shifted, lb_exp = sem("lb_shifted"), sem("lb_exp")
        f_soft, f_logsig, f_sig, fg_made, lf_made, b_made = (sem(n) for n in ("f_soft", "f_logsig", "f_sig", "fg_made", "lf_made", "b_made"))
        q_soft, q_logsig, q_sig, q_read = (sem(n) for n in ("q_soft", "q_logsig", "q_sig", "q_read"))
        eb_exp, kd_shifted, kd_exp, kd_made = (sem(n) for n in ("eb_exp", "kd_shifted", "kd_exp", "kd_made"))
        level_shifted, level_exp, level_made, level_mm, level_picked = (
            sem(n) for n in ("level_shifted", "level_exp", "level_made", "level_mm", "level_picked"))
        v_copied = sem("v_copied")
        gate_soft, gate_logsig, gate_sig, gate_read = (sem(n) for n in ("gate_soft", "gate_logsig", "gate_sig", "gate_read"))
        kd_turned, kd_copied, kv_mm, state_made, o_mm, o_squared, o_summed, o_rstd = (
            sem(n) for n in ("kd_turned", "kd_copied", "kv_mm", "state_made", "o_mm", "o_squared", "o_summed", "o_rstd"))
        r_done, y_ready, y_squared, y_summed, var_made, rstd_made, normed = (
            sem(n) for n in ("r_done", "y_ready", "y_squared", "y_summed", "var_made", "rstd_made", "normed"))
        y_added, y2_added = sem("y_added"), sem("y2_added")
        h_ready, h_squared, h_summed, h_rstd, t_made = (sem(n) for n in ("h_ready", "h_squared", "h_summed", "h_rstd", "t_made"))
        m_squared, m_summed, m_rstd, tm_made = (sem(n) for n in ("m_squared", "m_summed", "m_rstd", "tm_made"))
        u_read, a_silu = sem("u_read"), sem("a_silu")
        kv_copied, qb_copied, group_copied = sem("kv_copied"), sem("qb_copied"), sem("group_copied")
        s_mm, l_ready, p_exp, p_ready, p_turned, pt_ready, pv_mm = (
            sem(n) for n in ("s_mm", "l_ready", "p_exp", "p_ready", "p_turned", "pt_ready", "pv_mm"))
        n_squared, n_summed, n_rstd, n_made = (sem(n) for n in ("n_squared", "n_summed", "n_rstd", "n_made"))
        fox_v, vm_copied = sem("fox_v"), sem("vm_copied")
        sg_made, pu_read, pool_w_loaded = sem("sg_made"), sem("pu_read"), sem("pool_w_loaded")
        z_abs, z_exp, f_made, f_stored, f_bcast = (sem(n) for n in ("z_abs", "z_exp", "f_made", "f_stored", "f_bcast"))
        pooled, pool_mm = sem("pooled"), sem("pool_mm")
        out_ready, stored = sem("out_ready"), sem("stored")

        def wcols(slot):
            return (WH[slot][:, :].rearrange("p (k c) -> p k c", k=8), WL[slot][:, :].rearrange("p (k c) -> p k c", k=8))

        def wrows(slot):
            return (WH[slot][:, :].rearrange("p (k c) -> p k c", k=2), WL[slot][:, :].rearrange("p (k c) -> p k c", k=2))

        def halves(ap, m):
            return ap.rearrange("p h (n w m) -> p (h n) w m", w=2, m=m)

        SW_UNITS = [("sw", b, (2 * h, 2 * h + 1)) for b in range(4) for h in range(2)]
        LAST_UNITS = [("fox", j, (n,)) for j in range(4) for n in range(TT)] + \
                     [("mem", 4 + b, (2 * h, 2 * h + 1)) for b in range(2) for h in range(2)]
        U_LAST = 2 * len(SW_UNITS)

        def rows_of(unit, buf, slot):
            kind, _, tiles = unit
            if kind == "fox":
                return buf[:, slot, :, 0:(tiles[0] + 1) * P]
            if kind == "mem":
                return buf[:, slot].rearrange("p x (t s) -> p x t s", t=2)
            return buf[:, slot].rearrange("p (x t) s -> p x t s", t=2)

        def per_row(unit, small, slot):
            if unit[0] == "fox":
                return small[:, slot, 0:2]
            return small[:, slot].rearrange("p (x t) -> p x t", t=2)

        def ends_pair(units, i):
            return i >= 0 and (i + 1 == len(units) or units[i + 1][1] != units[i][1])

        block = ctx.enter_context(nc.Block())

        @block.sync
        def _(sp):
            def load(n, slot):
                sp.dma_start(RAW[slot][:, :], stream[n]).then_inc(w_loaded[slot], 16)

            for half in range(2):
                sp.dma_start(H[:, 4 * half:4 * half + 4], x_t[:, 4 * half:4 * half + 4]).then_inc(x_loaded[half], 16)
                load(half, half)
            with sp.Fori(0, (N_ALL - 2) // 2) as i:
                for slot in range(2):
                    sp.wait_ge(w_lo, 2 * i + slot + 1)
                    load(2 * i + (slot + 2), slot)
            if N_ALL % 2:
                sp.wait_ge(w_lo, N_ALL - 2)
                load(N_ALL - 1, (N_ALL - 1) % 2)

        @block.gpsimd
        def _(pool):
            def split_lo(n, slot):
                pool.wait_ge(w_hi, n + 1)
                pool.tensor_tensor(WL[slot][:, :], RAW[slot][:, :], WH[slot][:, :].bitcast(F32),
                                   ALU.subtract).then_inc(w_lo, 1)

            with pool.Fori(0, N_ALL // 2) as i:
                for slot in range(2):
                    split_lo(2 * i + slot, slot)
            if N_ALL % 2:
                split_lo(N_ALL - 1, (N_ALL - 1) % 2)

        @block.tensor
        def _(pe):
            def three(out_, wh, wl, xh, xl, start, stop):
                pe.matmul(out_, wh, xh, start=start, stop=False)
                pe.matmul(out_, wh, xl, start=False, stop=False)
                return pe.matmul(out_, wl, xh, start=False, stop=stop)

            def col_chunk(n, slot, banks, xh, xl, ms=(0, 1), ready=None, w=T, last=True, mid=None, ks=range(KB)):
                if ks[0] == 0:
                    pe.wait_ge(w_lo, n + 1)
                wh, wl = wcols(slot)
                for k in ks:
                    if mid and k == 3:
                        mid()
                    if ready:
                        pe.wait_ge(ready[0], ready[1] + k + 1)
                    for m in ms:
                        mm = three(banks[m][:, 0:w], wh[:, k, m * P:m * P + P], wl[:, k, m * P:m * P + P],
                                   xh[:, k], xl[:, k], k == 0, k == KB - 1)
                if last and ks[-1] == KB - 1:
                    mm.then_inc(w_used, 1)

            def tok_chunk(n, slot, outs, c0, c1, xh, xl, last=True, mid=None, ts=None):
                ts = ts or range(len(outs))
                if ts[0] == 0:
                    pe.wait_ge(w_lo, n + 1)
                wh, wl = wcols(slot)
                for t in ts:
                    if mid and t == 2:
                        mid()
                    for k in range(KB):
                        mm = three(outs[t], xh[:, k, t * P:t * P + P], xl[:, k, t * P:t * P + P],
                                   wh[:, k, c0:c1], wl[:, k, c0:c1], k == 0, k == KB - 1)
                if last and ts[-1] == len(outs) - 1:
                    mm.then_inc(w_used, 1)

            def row_chunk(n, slot, j, xh, xl, first, last, ms=range(8)):
                if ms[0] == 0:
                    pe.wait_ge(w_lo, n + 1)
                wh, wl = wrows(slot)
                for m in ms:
                    for k in range(2):
                        xk = bass.ds(2 * j + k, 1)
                        mm = three(bk(m), wh[:, k, m * P:m * P + P], wl[:, k, m * P:m * P + P],
                                   xh[:, xk].squeeze(1), xl[:, xk].squeeze(1), first and k == 0, last and k == 1)
                    if last and m < 7:
                        mm.then_inc(r_done, 1)
                if ms[-1] == 7:
                    mm.then_inc(w_used, 1)

            def layer_sums(idx):
                def add(b, what, start=False, stop=False):
                    return pe.matmul(bk(b), con["mean"], what, start=start, stop=stop)

                pe.wait_ge(y_added, idx + 1)
                add(0, SY[:, :], start=True)
                pe.wait_ge(y_ready, 8 * idx + 7)
                add(0, H[:, 6])
                pe.wait_ge(y2_added, 5 * idx + 5)
                add(1, SY2[:, :], start=True)
                pe.wait_ge(y_squared, 8 * idx + 6)
                add(1, SQ[:, 1])
                pe.wait_ge(y_ready, 8 * idx + 8)
                add(0, H[:, 7], stop=True).then_inc(y_summed, 1)
                pe.wait_ge(y_squared, 8 * idx + 7)
                add(1, SQ[:, 2])
                pe.wait_ge(y_squared, 8 * idx + 8)
                add(1, SQ[:, 3], stop=True).then_inc(y_summed, 1)

            def early_projection(n0, j, ready, count):
                pe.wait_ge(ready, count)
                row_chunk(n0 + j, (n0 + j) % 2, j, OH, OL, j == 0, False, ms=range(4))

            def out_projection(n0, count):
                pe.wait_ge(o_ready, count)
                for j in range(2):
                    row_chunk(n0 + j, (n0 + j) % 2, j, OH, OL, j == 0, False, ms=range(4, 8))
                for j in (2, 3):
                    row_chunk(n0 + j, (n0 + j) % 2, j, OH, OL, False, j == 3)

            def project_f(it, first=False):
                if not first:
                    pe.wait_ge(v_copied, it)
                col_chunk(N_HG + 4 * it, 0, (bk(0), bk(1)), AH, AL, ready=(a_ready, 0) if first else None)

            def hgrn(it, last):
                n = N_HG + 4 * it

                def level(lv):
                    s = lv % 2
                    if lv >= 2:
                        pe.wait_ge(level_picked, 8 * it + lv - 1)
                    if lv < LEVELS:
                        pe.wait_ge(level_made, 7 * it + lv + 1)
                    for h in range(2):
                        for c in range(TT):
                            cs = slice(c * P, c * P + P)
                            k_, q_ = (KT_[:, s, h, cs], QT[:, s, h, cs]) if lv < LEVELS else (KK[:, h, cs], QQ[:, h, cs])
                            mm = pe.matmul(bk(4 + 2 * s + h)[:, cs], k_, q_, start=True, stop=True)
                    mm.then_inc(level_mm, 1)

                pe.wait_ge(f_logsig, it + 1)
                vouts = [bk(i // 2)[:, 256 * (i % 2):256 * (i % 2) + 256] for i in range(TT)]
                tok_chunk(n + 2, 0, vouts, 0, 256, AH, AL, ts=(0, 1, 2))
                level(0)
                tok_chunk(n + 2, 0, vouts, 0, 256, AH, AL, ts=(3,))
                level(1)
                pe.wait_ge(q_read, it + 1)
                for k in range(6):
                    if k < 4:
                        col_chunk(n + 3, 1, (bk(2), bk(3)), AH, AL, ks=(2 * k, 2 * k + 1))
                    level(2 + k)
                pe.wait_ge(kd_made, it + 1)
                pe.wait_ge(level_picked, 8 * it + 7)
                for h in range(2):
                    for c in range(TT - 1):
                        mm = pe.transpose(bk(4 + h)[:, c * P:c * P + P], KD[:, h, c * P:c * P + P], con["ident"])
                mm.then_inc(kd_turned, 1)
                if not last:
                    project_f(it + 1)
                pe.wait_ge(kd_copied, it + 1)
                pe.wait_ge(v_copied, it + 1)
                pe.wait_ge(level_picked, 8 * it + 8)
                for h in range(2):
                    for c in range(TT - 1):
                        mm = pe.matmul(bk(6 + h)[:, c * P:c * P + P], QT[:, 0, h, c * P:c * P + P],
                                       VV[:, c, h * P:h * P + P], start=True, stop=True)
                mm.then_inc(kv_mm, 1)
                pe.wait_ge(state_made, it + 1)
                for h in range(2):
                    for c in range(TT):
                        cs = slice(c * P, c * P + P)
                        if c:
                            pe.matmul(bk(4 + h)[:, cs], BB[:, h, (c - 1) * P:c * P], QI[:, h, cs], start=True, stop=False)
                        mm = pe.matmul(bk(4 + h)[:, cs], VV[:, c, h * P:h * P + P], SS[:, h, c], start=c == 0, stop=True)
                mm.then_inc(o_mm, 1)

                def sums():
                    pe.wait_ge(o_squared, it + 1)
                    for h in range(2):
                        mm = pe.matmul(bk(6 + h), con["mean"], DD[:, 0, h], start=True, stop=True)
                    mm.then_inc(o_summed, 1)

                if last:
                    pe.wait_ge(v_copied, 4)
                    pe.wait_ge(gate_read, 4)
                    early_projection(N_HO, 0, o_ready, 2)
                    sums()
                    early_projection(N_HO, 1, o_ready, 4)
                else:
                    pe.wait_ge(gate_read, it + 1)
                    col_chunk(n + 5, 1, (bk(2), bk(3)), AH, AL, mid=sums)

            project_f(0, first=True)
            pe.wait_ge(rel_loaded, 32)
            pe.matmul(bk(7)[0:SWH, 0:2 * P], REL[:, 0:SWH], REL[:, SWH:SWH + 2 * P], start=True, stop=True).then_inc(rel_mm, 1)
            col_chunk(N_HG + 1, 1, (bk(2), bk(3)), AH, AL)
            pe.wait_ge(consts_in, 80)
            with pe.Fori(0, 3) as it:
                hgrn(it, False)
            hgrn(3, True)

            def ffn(layer, n_in, n_down, a_base):
                s0 = n_in % 2

                def pair(j):
                    n = n_in + 2 * j
                    pe.wait_ge(u_read, FB * layer + 2 * j - 1)
                    col_chunk(n, s0, (bk(0), bk(1)), AH, AL)
                    pe.wait_ge(u_read, FB * layer + 2 * j)
                    col_chunk(n + 1, 1 - s0, (bk(2), bk(3)), AH, AL)

                pieces = ((n_in, s0, (bk(0), bk(1))), (n_in + 1, 1 - s0, (bk(2), bk(3))))
                for k in range(4):
                    for n, s, banks in pieces:
                        col_chunk(n, s, banks, AH, AL, ready=(a_ready, a_base), ks=(k,))
                for n, s, banks in pieces:
                    col_chunk(n, s, banks, AH, AL, ready=(a_ready, a_base), ks=range(4, 8))
                with pe.Fori(1, FB // 2) as j:
                    pair(j)
                s0 = n_down % 2
                pe.wait_ge(u_read, FB * (layer + 1))

                def down(j, s, first=False, last=False):
                    pe.wait_ge(g_ready, 11 * layer + j + 1)
                    row_chunk(n_down + j, s, j, GH, GL, first, last)

                down(0, s0, first=True)
                with pe.Fori(0, 4) as i:
                    down(2 * i + 1, 1 - s0)
                    down(2 * i + 2, s0)
                down(9, 1 - s0)
                down(10, s0, last=True)

            out_projection(N_HO, 8)
            layer_sums(0)
            ffn(0, N_F0, N_D0, 8)
            layer_sums(1)

            def attend(u0, units, query, key, value, PL, PT, pair_free, early=None):
                def keys_of(unit, n):
                    return {"sw": (max(n - 1, 0), min(n + 1, 2)), "fox": (0, n + 1), "mem": (0, 2)}[unit[0]]

                def score(i):
                    kind, b, tiles = units[i]
                    s = i % 2
                    if i >= 2:
                        pe.wait_ge(l_ready, u0 + i - 1)
                    for t, n in enumerate(tiles):
                        k0, nk = keys_of(units[i], n)
                        for x in range(2):
                            if kind == "fox":
                                o = bk(2 * s + x)[:, 0:nk * P]
                            else:
                                o = bk(2 * s + x)[:, 256 * t + (2 - nk) * P:256 * t + 256]
                            mm = pe.matmul(o, query(b, n)[64 * x:64 * x + 64], key(b, k0, nk)[64 * x:64 * x + 64],
                                           start=True, stop=True)
                    mm.then_inc(s_mm, 1)

                def turn(i):
                    kind, b, tiles = units[i]
                    rows = rows_of(units[i], PL, i % 3)
                    pe.wait_ge(p_ready, u0 + i + 1)
                    if i:
                        pe.wait_ge(pt_ready, u0 + i)
                    for t in range(len(tiles)):
                        for x in range(2):
                            src = rows[:, x] if kind == "fox" else rows[:, x, t]
                            for kb in range(tiles[0] + 1 if kind == "fox" else 2):
                                at = x * 4 + 2 * t + kb
                                mm = pe.transpose(bk(4 + at // 4)[:, at % 4 * P:at % 4 * P + P],
                                                  src[:, kb * P:kb * P + P], con["ident"])
                    mm.then_inc(p_turned, 1)

                def weigh(i):
                    kind, b, tiles = units[i]
                    pe.wait_ge(pt_ready, u0 + i + 1)
                    if ends_pair(units, i - 1) and b >= 2:
                        pe.wait_ge(o_ready, pair_free + b - 1)
                    for t, n in enumerate(tiles):
                        k0, nk = keys_of(units[i], n)
                        for x in range(2):
                            for kb in range(nk):
                                at = x * 4 + kb if kind == "fox" else x * 4 + t * 2 + kb + 2 - nk
                                mm = pe.matmul(bk(6 + b % 2)[64 * x:64 * x + 64, n * P:n * P + P], value(b, k0 + kb, x),
                                               PT[:, i % 2, at], start=kb == 0, stop=kb == nk - 1)
                    mm.then_inc(pv_mm, 1)

                score(0)
                score(1)
                for i in range(len(units)):
                    if i + 2 < len(units):
                        score(i + 2)
                    if early and i == len(units) - 1:
                        pe.wait_ge(l_ready, u0 + len(units))
                        early(0)
                    turn(i)
                    if i:
                        weigh(i - 1)
                if early:
                    early(1)
                weigh(len(units) - 1)

            s0 = N_KV % 2
            col_chunk(N_KV, s0, (bk(2), bk(3)), AH, AL, ready=(a_ready, 16))
            tok_chunk(N_KV + 1, 1 - s0, [bk(4 + t // 2)[:, 256 * (t % 2):256 * (t % 2) + 256] for t in range(TT)], 0, 256, AH, AL)

            pe.wait_ge(kv_copied, 2)
            s0 = N_SQ % 2
            with pe.Fori(0, 2) as it:
                col_chunk(N_SQ + 2 * it, s0, (bk(0), bk(1)), AH, AL)
                col_chunk(N_SQ + 2 * it + 1, 1 - s0, (bk(2), bk(3)), AH, AL)
                pe.wait_ge(qb_copied, 2 * it + 2)
                pe.wait_ge(group_copied, it + 1)
                pe.wait_ge(o_ready, 8 + 4 * it)
                attend(8 * it, SW_UNITS,
                       lambda b, n: QB[:, b, n * P:n * P + P],
                       lambda b, k0, nk: KC[:, k0 * P:(k0 + nk) * P],
                       lambda b, t, x: VC[:, t, 64 * x:64 * x + 64], PL, PT, 8 + 4 * it)
            for j in range(2):
                early_projection(N_SO, j, o_ready, 10 + 2 * j)
            out_projection(N_SO, 16)
            layer_sums(2)
            ffn(1, N_F1, N_D1, 24)
            layer_sums(3)

            for m in range(KB):
                pe.wait_ge(h_squared, m + 1)
                pe.matmul(bk(2), con["mean"], SQ[:, m % 4], start=m == 0, stop=m == 7).then_inc(h_summed, 1)
                pe.wait_ge(m_squared, m + 1)
                pe.matmul(bk(3)[:, 0:MEM], con["mean"], TN[:, m, 0:MEM], start=m == 0, stop=m == 7).then_inc(m_summed, 1)
            s0 = N_MEM % 2
            col_chunk(N_MEM, s0, (bk(4), bk(5)), MH, ML, ready=(m_ready, 0), w=MEM)
            tok_chunk(N_MEM + 1, 1 - s0, [bk(6)[:, 256 * t:256 * t + 256] for t in range(2)], 0, 256, MH, ML)
            pe.wait_ge(n_squared, 1)
            pe.matmul(bk(7).rearrange("p (t c) -> p t c", t=2), con["mean64"], SQH[:, :, 0:MEM], start=True, stop=True).then_inc(n_summed, 1)
            col_chunk(N_FG, N_FG % 2, (bk(1),), AH, AL, ms=(0,), ready=(a_ready, 32))

            def head_norm(i):
                pe.wait_ge(n_squared, i + 1)
                for x in range(2):
                    mm = pe.matmul(bk(4 + x), con["mean64"], SQH[:, x], start=True, stop=True)
                mm.then_inc(n_summed, 1)

            pe.wait_ge(z_abs, 1)
            pe.wait_ge(n_made, 1)
            col_chunk(N_UA, N_UA % 2, (bk(0), bk(1)), AH, AL)
            col_chunk(N_QM, N_QM % 2, (bk(2), bk(3)), AH, AL)
            pe.wait_ge(pu_read, 1)
            col_chunk(N_GA, N_GA % 2, (bk(0), bk(1)), AH, AL, mid=lambda: head_norm(1))
            pe.wait_ge(pool_w_loaded, 16)
            pe.wait_ge(pooled, 1)
            pe.wait_ge(vm_copied, 1)
            for b in range(2):
                mm = pe.matmul(bk(6 + b), WP[:, b], PD[:, b], start=True, stop=True)
            mm.then_inc(pool_mm, 1)
            pe.wait_ge(n_made, 2)
            col_chunk(N_GM, N_GM % 2, (bk(2), bk(3)), AH, AL)

            s0 = N_FX % 2
            with pe.Fori(0, 4) as j:
                pe.wait_ge(n_made, j + 2)
                pe.wait_ge(sg_made, j + 1)
                col_chunk(N_FX + 2 * j, s0, (bk(0), bk(1)), AH, AL)
                pe.wait_ge(sg_made, j + 2)
                tok_chunk(N_FX + 2 * j + 1, 1 - s0, [bk(2)[:, t * P:t * P + P] for t in range(TT)], 0, P, AH, AL, last=False,
                          mid=lambda: head_norm(j + 2))
                col_chunk(N_FX + 2 * j + 1, 1 - s0, (None, bk(3)), AH, AL, ms=(1,))

            pe.wait_ge(n_made, 6)
            pe.wait_ge(fox_v, 4)
            pe.wait_ge(sg_made, 6)
            pe.wait_ge(o_ready, 18)
            attend(U_LAST, LAST_UNITS,
                   lambda b, n: (QKN[:, b, 0] if b < 4 else QMN[:, b - 4])[:, n * P:n * P + P],
                   lambda b, k0, nk: QKN[:, b, 1, 0:nk * P] if b < 4 else KM[:, b - 4],
                   lambda b, t, x: VF[:, b, t, 64 * x:64 * x + 64] if b < 4 else VM[:, t, (b - 4) * P + 64 * x:(b - 4) * P + 64 * x + 64],
                   PL2, PT2[:, :, :, :].rearrange("p s x (k c) -> p s (x k) c", c=P), 18,
                   lambda j: early_projection(N_OUT, j, o_ready, 18 + 2 * j))
            out_projection(N_OUT, 24)

        @block.scalar
        def _(act):
            def split_hi(n, slot, uses):
                if not (isinstance(n, int) and n >= N_ALL):
                    if not (isinstance(n, int) and n < 2):
                        act.wait_ge(w_used, n - 1)
                    act.wait_ge(w_loaded[slot], 16 * uses)
                    act.activation(WH[slot][:, :], RAW[slot][:, :], ACT.Copy).then_inc(w_hi, 1)

            def split_next(n):
                split_hi(n + 2, n % 2, (n + 2) // 2 + 1)

            def split_loop(b, step, i):
                split_hi(b + 2 + step * i, b % 2, (b + 2) // 2 + 1 + (step // 2) * i)

            act.preload_act_table_set("natural_log_exp_and_others")
            split_hi(0, 0, 1)
            split_hi(1, 1, 1)
            act.dma_start(PAR[:, :], params).then_inc(consts_in, 16)
            act.dma_start(CON[:, :], consts).then_inc(consts_in, 16)
            act.dma_start(MASK[:, :, :], masks).then_inc(consts_in, 16)
            act.dma_start(SINK[:, :], sinks_bcast).then_inc(consts_in, 16)
            act.dma_start(ROWM[:, :], rel_in[BUCKETS:BUCKETS + SWH, SWH:]).then_inc(consts_in, 16)
            act.dma_start(REL[:, 0:SWH], rel_in[0:BUCKETS, 0:SWH]).then_inc(rel_loaded, 16)
            act.dma_start(REL[:, SWH:], rel_in[0:BUCKETS, SWH:]).then_inc(rel_loaded, 16)
            act.wait_ge(lb_shifted, 1)
            act.activation(LB[:, 2:4], LB[:, 2:4], ACT.Exp).then_inc(lb_exp, 1)
            act.wait_ge(rows_made, 1)
            act.dma_start(bias_rows.rearrange("t h j -> h t j"),
                          ROWS[:, :].unsqueeze(1).broadcast_to([SWH, P, 2 * P])).then_inc(rows_stored, 16)
            act.wait_ge(rows_stored, 16)

            def rstd(out_, in_, scale, eps):
                act.activation(out_, in_, ACT.Ln, bias=eps, scale=scale)
                act.drain()
                return act.activation(out_, out_, ACT.Exp, scale=-0.5)

            def softplus(out_, z, done):
                act.activation(out_, z, ACT.Abs)
                act.drain()
                act.activation(out_, out_, ACT.Exp, scale=-1.0)
                act.drain()
                act.activation(out_, out_, ACT.Ln, bias=con["one"]).then_inc(done, 1)

            def exp_of(ap, done):
                act.activation(ap, ap, ACT.Exp).then_inc(done, 1)

            def front_f(it):
                act.wait_ge(w_used, N_HG + 1 + 4 * it)
                softplus(E1[:, :, :], bank[0][:, :, :], f_soft)
                split_loop(N_HG, 4, it)
                act.wait_ge(f_logsig, it + 1)
                exp_of(E1[:, :, :], f_sig)
                act.wait_ge(fg_made, it + 1)
                act.activation(EB[:, :, :], E1[:, :, :], ACT.Ln).then_inc(lf_made, 1)

            def front_q(it):
                act.wait_ge(level_shifted, 7 * it + 1)
                act.activation(DD[:, 0], DD[:, 0], ACT.Exp).then_inc(level_exp, 1)
                act.wait_ge(w_used, N_HG + 2 + 4 * it)
                softplus(E1[:, :, :], bank[1][:, :, :], q_soft)
                act.wait_ge(q_logsig, it + 1)
                exp_of(E1[:, :, :], q_sig)
                split_loop(N_HG + 1, 4, it)

            def decays(it):
                act.wait_ge(b_made, it + 1)
                act.activation(EB[:, :, :], BB[:, :, :], ACT.Exp).then_inc(eb_exp, 1)
                act.wait_ge(kd_shifted, it + 1)
                act.activation(KD[:, :, :], KD[:, :, :], ACT.Exp).then_inc(kd_exp, 1)

            def hgrn(it, last):
                for lv in range(1, LEVELS):
                    act.wait_ge(level_shifted, 7 * it + lv + 1)
                    act.activation(DD[:, lv % 2], DD[:, lv % 2], ACT.Exp).then_inc(level_exp, 1)
                    if lv == 5:
                        split_loop(N_HG + 2, 4, it)
                        act.activation(VV[:, :, :].rearrange("p (a b) c -> p a (b c)", a=2), bank[0][:, :, :], ACT.Copy).then_inc(v_copied, 1)
                act.wait_ge(kd_turned, it + 1)
                act.activation(QT[:, 0, :, 0:3 * P], bank[2][:, :, 0:3 * P], ACT.Copy).then_inc(kd_copied, 1)
                act.wait_ge(w_used, N_HG + 4 + 4 * it)
                softplus(E2[:, :, :], bank[1][:, :, :], gate_soft)
                split_loop(N_HG + 3, 4, it)
                act.wait_ge(gate_logsig, it + 1)
                exp_of(E2[:, :, :], gate_sig)
                if not last:
                    front_f(it + 1)
                act.wait_ge(o_mm, it + 1)
                act.activation(DD[:, 0], bank[2][:, :, :], ACT.Square).then_inc(o_squared, 1)
                if not last:
                    decays(it + 1)
                act.drain()
                act.wait_ge(o_summed, it + 1)
                rstd(DD[:, 1], bank[3][:, :, :], float(D // P), con["eps_rms"]).then_inc(o_rstd, 1)
                if not last:
                    front_q(it + 1)

            front_f(0)
            decays(0)
            front_q(0)
            with act.Fori(0, 3) as it:
                act.preload_act_table_set("natural_log_exp_and_others")
                hgrn(it, False)
            act.preload_act_table_set("natural_log_exp_and_others")
            hgrn(3, True)

            def squares(m):
                if m < 0:
                    act.wait_ge(mem_loaded, 16)
                    return
                act.wait_ge(h_ready, m + 1)
                if m >= 4:
                    act.wait_ge(h_summed, m - 3)
                act.activation(SQ[:, m % 4], H[:, m], ACT.Square).then_inc(h_squared, 1)
                act.activation(TN[:, m, 0:MEM], MT[:, m], ACT.Square).then_inc(m_squared, 1)

            def layer_norm(idx, g, b, split, n_last, load=None):
                for m in range(KB):
                    act.wait_ge(y_ready, 8 * idx + m + 1)
                    if m >= 4:
                        act.wait_ge(y2_added, 5 * idx + m - 3)
                    act.activation(SQ[:, m % 4], H[:, m], ACT.Square).then_inc(y_squared, 1)
                split_next(n_last)
                if load:
                    load()
                act.wait_ge(var_made, idx + 1)
                rstd(VAR[:, :], VAR[:, :], 1.0, con["eps_ln"]).then_inc(rstd_made, 1)
                for m in range(KB):
                    act.wait_ge(normed, 8 * idx + m + 1)
                    ins = act.activation(H[:, m], H[:, m], ACT.Identity, bias=b[:, m:m + 1], scale=g[:, m:m + 1])
                    if split:
                        act.drain()
                        act.activation(AH[:, m], H[:, m], ACT.Copy).then_inc(ah_ready, 1)
                    else:
                        ins.then_inc(h_ready, 1)
                        squares(m - 1)
                if not split:
                    squares(KB - 1)

            def ffn(n_in, n_down, layer):
                with act.Fori(0, FB // 2) as j:
                    act.preload_act_table_set("silu_and_others")
                    split_loop(n_in, 2, j)
                    act.wait_ge(u_read, FB * layer + 2 * j + 1)
                    act.activation(CB[:, :, :], CA[:, :, :], ACT.Silu).then_inc(a_silu, 1)
                    split_loop(n_in + 1, 2, j)
                split_next(n_down)
                with act.Fori(0, 4) as j:
                    act.preload_act_table_set("natural_log_exp_and_others")
                    split_loop(n_down + 1, 2, j)
                    split_loop(n_down + 2, 2, j)
                split_next(n_down + 9)

            act.preload_act_table_set("natural_log_exp_and_others")
            for j in range(3):
                split_next(N_HO + j)
            layer_norm(0, par["mix_g"][:, 0:8], par["mix_b"][:, 0:8], True, N_HO + 3)
            ffn(N_F0, N_D0, 0)
            act.preload_act_table_set("natural_log_exp_and_others")

            def load_bias():
                act.dma_start(BIAS[:, :, :], bias_toeplitz).then_inc(bias_loaded, 16)

            layer_norm(1, par["ffn_g"][:, 0:8], par["ffn_b"][:, 0:8], True, N_D0 + 10, load_bias)

            def attend(u0, units, PL, PT):
                def expo(i):
                    kind, _, tiles = units[i]
                    act.drain()
                    act.wait_ge(l_ready, u0 + i + 1)
                    s = i % 3
                    if kind == "sw":
                        act.activation(SNK[:, s], SNK[:, s], ACT.Exp)
                    rows = rows_of(units[i], PL, s)
                    for r in range(2 * len(tiles)):
                        row = rows[:, r] if kind == "fox" else rows[:, r // 2, r % 2]
                        ins = act.activation(row, row, ACT.Exp, bias=NMAX[:, s, r:r + 1], accum_out=SUMS[:, s, r:r + 1])
                    ins.then_inc(p_exp, 1)

                expo(0)
                for i, (kind, _, tiles) in enumerate(units):
                    if i + 1 < len(units):
                        expo(i + 1)
                    act.wait_ge(p_turned, u0 + i + 1)
                    if i >= 2:
                        act.wait_ge(pv_mm, u0 + i - 1)
                    w = (tiles[0] + 1) * P if kind == "fox" else T
                    act.activation(PT[:, i % 2, :, 0:w], bank[2][:, :, 0:w], ACT.Copy).then_inc(pt_ready, 1)

            split_next(N_KV)
            act.activation(KT[:, :, :], bank[1][:, :, :], ACT.Copy).then_inc(kv_copied, 1)
            split_next(N_KV + 1)
            act.activation(VT[:, :, :].rearrange("p (a b) c -> p a (b c)", a=2), bank[2][:, :, :], ACT.Copy).then_inc(kv_copied, 1)
            with act.Fori(0, 2) as it:
                act.preload_act_table_set("natural_log_exp_and_others")
                for h in range(2):
                    split_loop(N_SQ + h, 2, it)
                    act.activation(QB[:, 2 * h:2 * h + 2], bank[h][:, :, :], ACT.Copy).then_inc(qb_copied, 1)
                attend(8 * it, SW_UNITS, PL, PT[:, :, :, :].rearrange("p s (x k) c -> p s x (k c)", x=2))
            act.preload_act_table_set("natural_log_exp_and_others")
            for j in range(3):
                split_next(N_SO + j)
            layer_norm(2, par["mix_g"][:, 8:16], par["mix_b"][:, 8:16], True, N_SO + 3)
            ffn(N_F1, N_D1, 1)
            act.preload_act_table_set("natural_log_exp_and_others")

            def load_memory():
                act.dma_start(MT[:, :, :], mem_t).then_inc(mem_loaded, 16)
                act.dma_start(WP[:, :, :], w_pool).then_inc(pool_w_loaded, 16)

            layer_norm(3, par["ffn_g"][:, 8:16], par["ffn_b"][:, 8:16], False, N_D1 + 10, load_memory)

            act.wait_ge(h_summed, 8)
            act.drain()
            rstd(VAR[:, :], bk(2), 1.0, con["eps_rms"]).then_inc(h_rstd, 1)
            act.wait_ge(m_summed, 8)
            act.drain()
            rstd(MEAN[:, 0:MEM], bk(3)[:, 0:MEM], 1.0, con["eps_rms"]).then_inc(m_rstd, 1)
            for m in range(KB):
                act.wait_ge(tm_made, m + 1)
                act.activation(MH[:, m], MT[:, m], ACT.Copy).then_inc(mh_ready, 1)
            for m in range(KB):
                act.wait_ge(t_made, m + 1)
                act.activation(AH[:, m], TN[:, m], ACT.Copy).then_inc(ah_ready, 1)

            def head_rstd(i, in_, w):
                act.drain()
                act.wait_ge(n_summed, i + 1)
                rstd(RH[:, :, 0:w], in_, 1.0, con["eps_rms"]).then_inc(n_rstd, 1)

            split_next(N_MEM)
            act.activation(SQH[:, :, 0:MEM], bank[2][:, :, 0:MEM], ACT.Square).then_inc(n_squared, 1)
            split_next(N_MEM + 1)
            act.activation(VM[:, :, :], bk(6).rearrange("p (t c) -> p t c", t=2), ACT.Copy).then_inc(vm_copied, 1)
            head_rstd(0, bk(7).rearrange("p (t c) -> p t c", t=2), MEM)
            split_next(N_FG)
            act.wait_ge(z_abs, 1)
            act.activation(FG_[:, 1], FG_[:, 1], ACT.Exp, scale=-1.0)
            act.drain()
            act.activation(FG_[:, 1], FG_[:, 1], ACT.Ln, bias=con["one"][0:8]).then_inc(z_exp, 1)
            act.wait_ge(f_made, 1)
            act.dma_start(forget_rows, FG_[:, 3]).then_inc(f_stored, 16)
            split_next(N_UA)
            act.wait_ge(w_used, N_QM + 1)
            act.activation(SQH[:, :, :], bank[1][:, :, :], ACT.Square).then_inc(n_squared, 1)
            split_next(N_QM)
            head_rstd(1, bank[2][:, :, :], T)
            act.wait_ge(w_used, N_GA + 1)
            act.activation(SG[:, 0:2], bank[0][:, :, :], ACT.Silu).then_inc(sg_made, 1)
            split_next(N_GA)
            act.wait_ge(f_stored, 16)
            act.dma_start(FBC[:, :, :], forget_bcast).then_inc(f_bcast, 16)
            act.wait_ge(w_used, N_GM + 1)
            act.activation(SG[:, 6:8], bank[1][:, :, :], ACT.Silu).then_inc(sg_made, 1)
            split_next(N_GM)

            with act.Fori(0, 4) as j:
                act.preload_act_table_set("natural_log_exp_and_others")
                act.wait_ge(w_used, N_FX + 1 + 2 * j)
                act.activation(SQH[:, :, :], bank[0][:, :, :], ACT.Square).then_inc(n_squared, 1)
                split_loop(N_FX, 2, j)
                head_rstd(j + 2, bank[2][:, :, :], T)
                act.wait_ge(w_used, N_FX + 2 + 2 * j)
                one_j = bass.ds(j, 1)
                act.activation(VF[:, one_j].squeeze(1), bk(2).rearrange("p (t c) -> p t c", t=TT), ACT.Copy).then_inc(fox_v, 1)
                act.activation(SG[:, bass.ds(j + 2, 1)].squeeze(1), bk(3), ACT.Silu).then_inc(sg_made, 1)
                split_loop(N_FX + 1, 2, j)
            act.preload_act_table_set("natural_log_exp_and_others")
            attend(U_LAST, LAST_UNITS, PL2, PT2)
            for j in range(4):
                split_next(N_OUT + j)
            for m in range(KB):
                act.wait_ge(out_ready, m + 1)
                act.dma_start(out[:, m], H[:, m]).then_inc(stored, 16)
            act.wait_ge(stored, 16 * KB)

        @block.vector
        def _(dve):
            def log_sigmoid(ap, z, done):
                dve.scalar_tensor_tensor(ap, z, 0.0, ap, ALU.min, ALU.subtract).then_inc(done, 1)

            for m in range(KB):
                if m % 4 == 0:
                    dve.wait_ge(x_loaded[m // 4], 16)
                dve.tensor_copy(AH[:, m], H[:, m])
                dve.drain()
                dve.tensor_tensor(AL[:, m], H[:, m], AH[:, m].bitcast(F32), ALU.subtract).then_inc(a_ready, 1)
            dve.wait_ge(consts_in, 80)
            lb = par["lb"].rearrange("p (l h) -> p l h", l=2)
            dve.tensor_tensor(LB[:, 0], lb[:, 0], lb[:, 1], ALU.max)
            dve.drain()
            for i in range(2):
                ins = dve.tensor_tensor(LB[:, 2 + i], lb[:, i], LB[:, 0], ALU.subtract)
            ins.then_inc(lb_shifted, 1)
            dve.wait_ge(rel_mm, 1)
            dve.tensor_tensor(ROWS[:, :], bk(7)[0:SWH, 0:2 * P], ROWM[:, :], ALU.add).then_inc(rows_made, 1)
            dve.wait_ge(lb_exp, 1)
            dve.tensor_tensor(LB[:, 1], LB[:, 2], LB[:, 3], ALU.add)
            dve.drain()
            dve.reciprocal(LB[:, 1], LB[:, 1])
            dve.drain()
            dve.tensor_tensor(LB[:, 0], LB[:, 2], LB[:, 1], ALU.mult)
            dve.drain()
            dve.tensor_scalar(LB[:, 1], LB[:, 0], -1.0, 1.0, ALU.mult, ALU.add)
            dve.wait_ge(rows_stored, 16)
            dve.memset(SS[:, :, :, :], 0.0)
            dve.memset(QT[:, :, :, :], 0.0)
            dve.memset(KT_[:, :, :, :], 0.0)
            dve.drain()

            def front_f(it, later):
                dve.wait_ge(f_soft, it + 1)
                log_sigmoid(E1[:, :, :], bank[0][:, :, :], f_logsig)
                dve.wait_ge(f_sig, it + 1)
                for h in range(2):
                    col = bass.ds(2 * it + h, 1)
                    dve.tensor_scalar(E1[:, h], E1[:, h], LB[:, 1, col], LB[:, 0, col], ALU.mult, ALU.add)
                dve.drain()
                dve.tensor_scalar(KK[:, :, :], E1[:, :, :], -1.0, 1.0, ALU.mult, ALU.add)
                dve.drain()
                dve.tensor_scalar(E1[:, :, :], E1[:, :, :], TINY, None, ALU.max).then_inc(fg_made, 1)
                dve.wait_ge(lf_made, it + 1)
                if later:
                    dve.wait_ge(o_mm, it)
                for h in range(2):
                    ins = dve.tensor_tensor_scan(BB[:, h], con["carry"], EB[:, h], 0.0, ALU.mult, ALU.add)
                ins.then_inc(b_made, 1)
                dve.drain()
                B4 = BB[:, :, :].rearrange("p h (c t) -> p (h c) t", t=P)
                dve.tensor_tensor(KD[:, :, :].rearrange("p h (c t) -> p (h c) t", t=P),
                                  B4[:, :, P - 1:P].broadcast_to([P, 8, P]), B4, ALU.subtract).then_inc(kd_shifted, 1)

            def shift(lv):
                m = 64 >> lv
                b4, d4 = halves(BB[:, :, :], m), halves(DD[:, lv % 2], m)
                mid = b4[:, :, 0, m - 1:m].broadcast_to([P, 2 * T // (2 * m), m])
                dve.tensor_tensor(d4[:, :, 1], b4[:, :, 1], mid, ALU.subtract)
                dve.tensor_tensor(d4[:, :, 0], mid, b4[:, :, 0], ALU.subtract).then_inc(level_shifted, 1)

            def front_q(it):
                shift(0)
                dve.drain()
                dve.wait_ge(q_soft, it + 1)
                log_sigmoid(E1[:, :, :], bank[1][:, :, :], q_logsig)
                dve.wait_ge(q_sig, it + 1)
                dve.tensor_tensor(QQ[:, :, :], bank[1][:, :, :], E1[:, :, :], ALU.mult).then_inc(q_read, 1)

            def hgrn(it, last):
                def scale_qk(lv):
                    m = 64 >> lv
                    dve.wait_ge(level_exp, 7 * it + lv + 1)
                    d4 = halves(DD[:, lv % 2], m)
                    dve.tensor_tensor(halves(QT[:, lv % 2], m)[:, :, 1], halves(QQ[:, :, :], m)[:, :, 1], d4[:, :, 1], ALU.mult)
                    dve.tensor_tensor(halves(KT_[:, lv % 2], m)[:, :, 0], halves(KK[:, :, :], m)[:, :, 0], d4[:, :, 0],
                                      ALU.mult).then_inc(level_made, 1)

                def pick(lv):
                    dve.wait_ge(level_mm, 8 * it + lv + 1)
                    dve.memset(PAD[:, :], 0.0)
                    for h in range(2):
                        ins = dve.copy_predicated(SS[:, h], MASK[:, lv:lv + 1].bitcast(U32).broadcast_to([P, TT, P]),
                                                  bk(4 + 2 * (lv % 2) + h).rearrange("p (c t) -> p c t", t=P))
                    ins.then_inc(level_picked, 1)

                for st in range(1, LEVELS + 4):
                    dve.drain()
                    if st == 1:
                        scale_qk(0)
                    if st < LEVELS:
                        shift(st)
                    if st == 2:
                        dve.wait_ge(eb_exp, it + 1)
                        dve.tensor_tensor(QI[:, :, :], QQ[:, :, :], EB[:, :, :], ALU.mult)
                    if st == 3:
                        dve.wait_ge(kd_exp, it + 1)
                        dve.tensor_tensor(KD[:, :, :], KD[:, :, :], KK[:, :, :], ALU.mult).then_inc(kd_made, 1)
                    if 3 <= st:
                        pick(st - 3)
                    if 2 <= st <= LEVELS:
                        scale_qk(st - 1)
                dve.wait_ge(gate_soft, it + 1)
                log_sigmoid(E2[:, :, :], bank[1][:, :, :], gate_logsig)
                dve.wait_ge(gate_sig, it + 1)
                dve.tensor_tensor(E2[:, :, :], E2[:, :, :], bank[1][:, :, :], ALU.mult).then_inc(gate_read, 1)
                dve.drain()
                dve.wait_ge(kv_mm, it + 1)
                dve.tensor_copy(BB[:, :, 0:P], bank[3][:, :, 0:P])
                for c in range(1, TT - 1):
                    dve.drain()
                    for h in range(2):
                        ins = dve.scalar_tensor_tensor(BB[:, h, c * P:c * P + P], BB[:, h, (c - 1) * P:c * P],
                                                       EB[:, h, c * P + P - 1:c * P + P], bk(6 + h)[:, c * P:c * P + P],
                                                       ALU.mult, ALU.add)
                ins.then_inc(state_made, 1)
                if not last:
                    dve.drain()
                    front_f(it + 1, True)
                dve.wait_ge(o_rstd, it + 1)
                dve.tensor_tensor(DD[:, 1], bank[2][:, :, :], DD[:, 1], ALU.mult)
                dve.drain()
                dve.scalar_tensor_tensor(DD[:, 1], DD[:, 1], par["gnorm"], E2[:, :, :], ALU.mult, ALU.mult)
                dve.drain()
                for h in range(2):
                    dve.tensor_copy(OH[:, bass.ds(2 * it + h, 1)].squeeze(1), DD[:, 1, h])
                dve.drain()
                for h in range(2):
                    col = bass.ds(2 * it + h, 1)
                    dve.tensor_tensor(OL[:, col].squeeze(1), DD[:, 1, h], OH[:, col].squeeze(1).bitcast(F32), ALU.subtract).then_inc(o_ready, 1)
                dve.drain()
                if not last:
                    front_q(it + 1)
                    dve.drain()

            front_f(0, False)
            front_q(0)
            dve.drain()
            with dve.Fori(0, 3) as it:
                hgrn(it, False)
            hgrn(3, True)

            def layer_norm(idx, n_last, split):
                for m in range(KB):
                    if m < 7:
                        dve.wait_ge(r_done, 7 * idx + m + 1)
                    else:
                        dve.wait_ge(w_used, n_last + 1)
                    dve.scalar_tensor_tensor(H[:, m], H[:, m], ALPHA, bk(m), ALU.mult, ALU.add).then_inc(y_ready, 1)
                    if 1 <= m <= 5:
                        dve.drain()
                        ins = dve.tensor_tensor(SY[:, :], H[:, 0] if m == 1 else SY[:, :], H[:, m], ALU.add)
                        if m == 5:
                            ins.then_inc(y_added, 1)
                        dve.wait_ge(y_squared, 8 * idx + m)
                        if m == 1:
                            dve.tensor_copy(SY2[:, :], SQ[:, 0]).then_inc(y2_added, 1)
                        else:
                            dve.tensor_tensor(SY2[:, :], SY2[:, :], SQ[:, (m - 1) % 4], ALU.add).then_inc(y2_added, 1)
                dve.drain()
                dve.wait_ge(y_summed, 2 * idx + 1)
                dve.tensor_copy(MEAN[:, :], bk(0))
                dve.drain()
                dve.tensor_tensor(VAR[:, :], MEAN[:, :], MEAN[:, :], ALU.mult)
                dve.drain()
                dve.wait_ge(y_summed, 2 * idx + 2)
                dve.tensor_tensor(VAR[:, :], bk(1), VAR[:, :], ALU.subtract)
                dve.drain()
                dve.tensor_scalar(VAR[:, :], VAR[:, :], 0.0, None, ALU.max).then_inc(var_made, 1)

                def centre(m):
                    dve.tensor_tensor(H[:, m], H[:, m], MEAN[:, :], ALU.subtract)

                def low(m):
                    dve.wait_ge(ah_ready, 8 * idx + m + 1)
                    dve.tensor_tensor(AL[:, m], H[:, m], AH[:, m].bitcast(F32), ALU.subtract).then_inc(a_ready, 1)

                centre(0)
                centre(1)
                dve.wait_ge(rstd_made, idx + 1)
                for m in range(KB):
                    dve.drain()
                    dve.tensor_tensor(H[:, m], H[:, m], VAR[:, :], ALU.mult).then_inc(normed, 1)
                    if m + 2 < KB:
                        centre(m + 2)
                    if split and m >= 2:
                        low(m - 2)
                if split:
                    low(6)
                    low(7)

            def ffn(layer, n_in):
                def conv(out_, src, ab, j):
                    for c in range(2):
                        blk = bass.ds(2 * j + c, 1)
                        tap = [CONVW[:, layer, t, ab, blk] for t in range(3)]
                        dve.tensor_scalar(out_[:, c], src[:, c], tap[2], CONVB[:, layer, ab, blk], ALU.mult, ALU.add)
                    for d in (1, 2):
                        dve.drain()
                        for c in range(2):
                            blk = bass.ds(2 * j + c, 1)
                            ins = dve.scalar_tensor_tensor(out_[:, c, d:T], src[:, c, 0:T - d], CONVW[:, layer, 2 - d, ab, blk],
                                                           out_[:, c, d:T], ALU.mult, ALU.add)
                    return ins

                with dve.Fori(0, FB // 2) as j:
                    dve.drain()
                    dve.wait_ge(w_used, n_in + 1 + 2 * j)
                    conv(CA, bank[0], 0, j).then_inc(u_read, 1)
                    dve.drain()
                    dve.wait_ge(a_silu, 11 * layer + j + 1)
                    dve.wait_ge(w_used, n_in + 2 + 2 * j)
                    conv(CA, bank[1], 1, j).then_inc(u_read, 1)
                    dve.drain()
                    dve.tensor_tensor(CA[:, :, :], CA[:, :, :], CB[:, :, :], ALU.mult)
                    dve.drain()
                    pair = bass.ds(2 * j, 2)
                    dve.tensor_copy(GH[:, pair], CA[:, :, :])
                    dve.drain()
                    dve.tensor_tensor(GL[:, pair], CA[:, :, :], GH[:, pair].bitcast(F32), ALU.subtract).then_inc(g_ready, 1)

            layer_norm(0, N_HO + 3, True)
            ffn(0, N_F0)
            layer_norm(1, N_D0 + 10, True)

            def attend(u0, units, PL, first_stage, finish, sink):
                def logits(i):
                    u, s = units[i], i % 3
                    rows, nmax = rows_of(u, PL, s), per_row(u, NMAX, s)
                    dve.drain()
                    dve.wait_ge(s_mm, u0 + i + 1)
                    if i >= 3:
                        dve.wait_ge(p_turned, u0 + i - 2)
                    if u[0] == "fox":
                        first_stage(u, bank[i % 2][:, :, 0:(u[2][0] + 1) * P], rows)
                    else:
                        first_stage(u, bank[i % 2][:, :, :].rearrange("p x (t s) -> p x t s", t=2), rows)
                    dve.drain()
                    ins = dve.tensor_reduce(nmax, rows, AX_X, ALU.max, negate=True)
                    if sink is not None:
                        dve.drain()
                        of_rows = sink(u[1]).unsqueeze(2).broadcast_to([P, 2, 2])
                        dve.scalar_tensor_tensor(nmax, of_rows, -1.0, nmax, ALU.mult, ALU.min)
                        dve.drain()
                        ins = dve.tensor_tensor(per_row(u, SNK, s), of_rows, nmax, ALU.add)
                    ins.then_inc(l_ready, 1)

                def end_pair(i):
                    if ends_pair(units, i):
                        dve.drain()
                        dve.wait_ge(pv_mm, u0 + i + 1)
                        finish(units[i][1])

                logits(0)
                for i, u in enumerate(units):
                    s, n_rows = i % 3, 2 * len(u[2])
                    if i + 1 < len(units):
                        logits(i + 1)
                    end_pair(i - 2)
                    dve.wait_ge(p_exp, u0 + i + 1)
                    if sink is not None:
                        dve.tensor_tensor(SUMS[:, s], SUMS[:, s], SNK[:, s], ALU.add)
                        dve.drain()
                    dve.reciprocal(RDEN[:, s, 0:n_rows], SUMS[:, s, 0:n_rows])
                    dve.drain()
                    rows = rows_of(u, PL, s)
                    for r in range(n_rows):
                        row = rows[:, r] if u[0] == "fox" else rows[:, r // 2, r % 2]
                        ins = dve.tensor_scalar(row, row, RDEN[:, s, r:r + 1], None, ALU.mult)
                    ins.then_inc(p_ready, 1)
                end_pair(len(units) - 2)
                end_pair(len(units) - 1)

            dve.wait_ge(kv_copied, 2)
            dve.wait_ge(bias_loaded, 16)
            SINK3 = SINK[:, :].rearrange("p (o x b) -> p o x b", o=2, x=2)
            BIAS5 = BIAS[:, :, :].rearrange("p (o x b) s -> p o x b s", o=2, x=2)
            with dve.Fori(0, 2) as it:
                one_it = bass.ds(it, 1)
                dve.tensor_copy(KC[:, :], KT[:, one_it].squeeze(1))
                dve.tensor_copy(VC[:, :, :], VT[:, :, bass.ds(it * P, P)]).then_inc(group_copied, 1)

                def sw_logits(u, src, dst):
                    bias = BIAS5[:, one_it, :, u[1]].squeeze(1)
                    first = u[2][0] == 0
                    if first:
                        dve.memset(dst[:, :, 0, 0:P], NEG)
                    for t in range(2):
                        lo = P if first and t == 0 else 0
                        dve.scalar_tensor_tensor(dst[:, :, t, lo:], src[:, :, t, lo:], SCALE, bias[:, :, lo:], ALU.mult, ALU.add)

                def sw_finish(b):
                    o = bk(6 + b % 2)
                    col = bass.ds(4 * it + b, 1)
                    dve.tensor_copy(OH[:, col].squeeze(1), o)
                    dve.drain()
                    dve.tensor_tensor(OL[:, col].squeeze(1), o, OH[:, col].squeeze(1).bitcast(F32), ALU.subtract).then_inc(o_ready, 1)

                attend(8 * it, SW_UNITS, PL, sw_logits, sw_finish, lambda b: SINK3[:, one_it, :, b].squeeze(1))
            layer_norm(2, N_SO + 3, True)
            ffn(1, N_F1)
            layer_norm(3, N_D1 + 10, False)

            dve.wait_ge(m_rstd, 1)
            for m in range(KB):
                dve.scalar_tensor_tensor(MT[:, m], MT[:, m], par["mem_g"][:, m:m + 1], MEAN[:, 0:MEM],
                                         ALU.mult, ALU.mult).then_inc(tm_made, 1)
            for m in range(KB):
                dve.wait_ge(mh_ready, m + 1)
                dve.tensor_tensor(ML[:, m], MT[:, m], MH[:, m].bitcast(F32), ALU.subtract).then_inc(m_ready, 1)
            dve.wait_ge(h_rstd, 1)
            for m in range(KB + 2):
                if m < KB:
                    dve.scalar_tensor_tensor(TN[:, m], H[:, m], par["norm_g"][:, m:m + 1], VAR[:, :],
                                             ALU.mult, ALU.mult).then_inc(t_made, 1)
                if m >= 2:
                    dve.wait_ge(ah_ready, 24 + m - 1)
                    dve.tensor_tensor(AL[:, m - 2], TN[:, m - 2], AH[:, m - 2].bitcast(F32), ALU.subtract).then_inc(a_ready, 1)

            def head_norm(i, src, gains, out_, w):
                dve.wait_ge(n_rstd, i + 1)
                for x in range(2):
                    ins = dve.scalar_tensor_tensor(out_[:, x, 0:w], src[:, x, 0:w], gains[x], RH[:, x, 0:w], ALU.mult, ALU.mult)
                ins.then_inc(n_made, 1)

            head_norm(0, bank[2], (par["mem_kg"], par["mem_kg"]), KM, MEM)
            dve.wait_ge(w_used, N_FG + 1)
            dve.tensor_scalar(FG_[:, 0], bk(1)[0:8], par["forget_b"][0:8], None, ALU.add)
            dve.drain()
            dve.scalar_tensor_tensor(FG_[:, 1], FG_[:, 0], -1.0, FG_[:, 0], ALU.mult, ALU.max).then_inc(z_abs, 1)
            dve.tensor_scalar(FG_[:, 2], FG_[:, 0], 0.0, None, ALU.min)
            dve.wait_ge(z_exp, 1)
            dve.drain()
            dve.tensor_tensor(FG_[:, 2], FG_[:, 2], FG_[:, 1], ALU.subtract)
            dve.drain()
            dve.tensor_tensor_scan(FG_[:, 3], con["one"][0:8].broadcast_to([8, T]), FG_[:, 2], 0.0, ALU.mult, ALU.add).then_inc(f_made, 1)

            dve.wait_ge(w_used, N_UA + 1)
            dve.tensor_copy(PU[:, :, :], bank[0][:, :, :]).then_inc(pu_read, 1)
            dve.drain()

            def widen(dst, src, b, lo, d):
                dve.tensor_copy(dst[lo:P, b, 0:d], src[lo:P, b, 0:d])
                dve.tensor_tensor(dst[lo:P, b, d:T], src[lo:P, b, d:T], src[lo:P, b, 0:T - d], ALU.add)

            widen(PS, PU, 0, 0, 1)
            widen(PS, PU, 1, 0, 1)
            dve.drain()
            dve.tensor_copy(PD[0:64, 0], PS[0:64, 0])
            widen(PD, PS, 0, 64, 2)
            widen(PD, PS, 1, 0, 2)
            dve.drain()
            widen(PS, PD, 1, 0, 4)
            dve.drain()
            dve.tensor_copy(PD[0:64, 1], PS[0:64, 1])
            widen(PD, PS, 1, 64, 8)
            dve.drain()
            inv = con["inv_count"].rearrange("p (b t) -> p b t", b=2)
            dve.tensor_tensor(PD[:, :, :], PD[:, :, :], inv, ALU.mult)
            dve.drain()
            dve.tensor_tensor(PD[:, :, :], PD[:, :, :], PU[:, :, :], ALU.subtract).then_inc(pooled, 1)
            head_norm(1, bank[1], (par["mem_qg"], par["mem_qg"]), QMN, T)
            dve.wait_ge(pool_mm, 1)
            dve.wait_ge(sg_made, 1)
            for b in range(2):
                dve.scalar_tensor_tensor(TP[:, :], bk(6 + b), par["pool_scale"][:, b:b + 1], SG[:, b], ALU.mult, ALU.mult)
                dve.drain()
                dve.tensor_copy(OH[:, b], TP[:, :])
                dve.drain()
                dve.tensor_tensor(OL[:, b], TP[:, :], OH[:, b].bitcast(F32), ALU.subtract).then_inc(o_ready, 1)
                dve.drain()

            with dve.Fori(0, 4) as j:
                head_norm(j + 2, bank[0], (par["fox_qg"], par["fox_kg"]), QKN[:, bass.ds(j, 1)].squeeze(1), T)

            def last_logits(u, src, dst):
                kind, b, tiles = u
                if kind == "mem":
                    dve.tensor_scalar(dst, src, SCALE, None, ALU.mult)
                    return
                w = (tiles[0] + 1) * P
                dve.scalar_tensor_tensor(dst, src, SCALE, FBC[:, 2 * b:2 * b + 2, 0:w], ALU.mult, ALU.subtract)
                dve.drain()
                diag = dst[:, :, w - P:w]
                dve.tensor_tensor(diag, diag, con["causal"].unsqueeze(1).broadcast_to([P, 2, P]), ALU.add)

            def gated(b):
                dve.tensor_tensor(TO[:, :], bk(6 + b % 2), SG[:, 2 + b], ALU.mult)
                dve.drain()
                dve.tensor_copy(OH[:, 2 + b], TO[:, :])
                dve.drain()
                dve.tensor_tensor(OL[:, 2 + b], TO[:, :], OH[:, 2 + b].bitcast(F32), ALU.subtract).then_inc(o_ready, 1)

            dve.wait_ge(f_bcast, 16)
            dve.wait_ge(sg_made, 6)
            attend(U_LAST, LAST_UNITS, PL2, last_logits, gated, None)
            dve.drain()
            for m in range(KB):
                if m < 7:
                    dve.wait_ge(r_done, 28 + m + 1)
                else:
                    dve.wait_ge(w_used, N_ALL)
                dve.tensor_tensor(H[:, m], H[:, m], bk(m), ALU.add).then_inc(out_ready, 1)


def col_chunks(w, cols):
    out = []
    for parts in cols:
        c = np.concatenate([w[:, a:b] for a, b in parts], axis=1)
        if c.shape[1] < 256:
            c = np.concatenate([c, np.zeros((c.shape[0], 256 - c.shape[1]), c.dtype)], axis=1)
        out.append(c.reshape(8, P, 256).transpose(1, 0, 2).reshape(1, P, 2048))
    return out


def row_chunks(w):
    n = w.shape[0] // 256
    return [w.reshape(n, 2, P, 1024).transpose(0, 2, 1, 3).reshape(n, P, 2048)]


def per_feature(a):
    n = a.shape[-1] // P
    return np.moveaxis(a.reshape(*a.shape[:-1], n, P), -1, 0).reshape(P, -1)


def constants():
    c = np.zeros((P, NCON), np.float32)
    i = np.arange(P)

    def put(name, v):
        a, b = CCOL[name]
        c[:, a:b] = v

    put("ident", np.eye(P))
    put("mean", 1.0 / D)
    put("mean64", (i[:, None] // 64 == i[None, :] // 64) / 64.0)
    put("causal", np.where(i[None, :] <= i[:, None], 0.0, NEG))
    put("carry", (np.arange(T) % P != 0).astype(np.float32)[None])
    put("eps_ln", LN_EPS)
    put("eps_rms", RMS_EPS)
    put("one", 1.0)
    win = np.array(POOL_WINDOWS)[(i[:, None] // 64) + 2 * np.arange(2)[None]]
    put("inv_count", (1.0 / np.minimum(np.arange(T)[None, None] + 1, win[:, :, None])).reshape(P, -1))
    masks = np.zeros((P, 8, P), np.float32)
    s, t = i[:, None], i[None, :]
    for lv in range(LEVELS):
        m = 64 >> lv
        masks[:, lv] = (s // (2 * m) == t // (2 * m)) & (s % (2 * m) < m) & (t % (2 * m) >= m)
    masks[:, 7] = s == t
    j = np.arange(2 * P)
    dist = P - j
    ok = (dist >= 0) & (dist < P)
    dc = np.clip(dist, 0, P - 1)
    d = np.maximum(dc, 1).astype(np.float32)
    log_b = 16 + (np.log(d / np.float32(16)) / np.float32(np.log(8.0)) * 16).astype(np.int32)
    bucket = np.where(dc < 16, dc, np.minimum(log_b, BUCKETS - 1))
    hot = ((bucket[None] == np.arange(BUCKETS)[:, None]) & ok[None]).astype(np.float32)
    return c, masks, hot, np.where(ok, 0.0, NEG).astype(np.float32)


def kernel(**inputs):
    import concourse.bacc as bacc
    from concourse.bass_utils import run_bass_kernel_spmd

    a = {k: np.asarray(v) for k, v in inputs.items()}
    con, masks, hot, row_mask = constants()
    parts = []
    w = a["hgrn_w_in"][0]
    for hp in range(4):
        for base in (1024, 0, 2048, 3072):
            parts += col_chunks(w, [[(base + 256 * hp, base + 256 * hp + 256)]])
    parts += row_chunks(a["hgrn_w_out"][0])
    ffn_in = [[[(256 * j, 256 * j + 256)], [(FFN + 256 * j, FFN + 256 * j + 256)]] for j in range(FB // 2)]
    heads = [8 * o + b + 4 * x for o in range(2) for b in range(4) for x in range(2)]
    for layer in range(2):
        if layer == 1:
            parts += col_chunks(a["shared_w_kv"], [[(0, 256)], [(256, 512)]])
            parts += col_chunks(a["swa_w_q"][0], [[(64 * h, 64 * h + 64) for h in heads[4 * c:4 * c + 4]] for c in range(4)])
            wo = a["swa_w_out"][0]
            parts += row_chunks(np.concatenate([wo[64 * h:64 * h + 64] for h in heads], axis=0))
        for pair in ffn_in:
            parts += col_chunks(a["ffn_w_in"][layer], pair)
        parts += row_chunks(a["ffn_w_out"][layer])
    parts += col_chunks(a["w_mem_kv_2"][0], [[(0, 256)], [(256, 512)]])
    w = a["w_in_2"][0]
    ua, ga, qb, kb, vb, fb, gb, qm, gm = np.cumsum([0, 256, 256, 512, 512, 512, 8, 512, 256])
    parts += col_chunks(w, [[(fb, fb + 8)]])
    parts += col_chunks(w, [[(c, c + 256)] for c in (ua, qm, ga, gm)])
    for j in range(4):
        parts += col_chunks(w, [[(qb + P * j, qb + P * j + P), (kb + P * j, kb + P * j + P)],
                                [(vb + P * j, vb + P * j + P), (gb + P * j, gb + P * j + P)]])
    parts += row_chunks(a["w_out_2"][0])
    stream = np.concatenate(parts, axis=0)

    def twice(v):
        return np.concatenate([v, v]).reshape(P, 1)

    vec = {
        "lb": per_feature(a["hgrn_lb_logits"]), "gnorm": a["hgrn_gnorm_w"].reshape(P, 1),
        "conv_w": per_feature(a["ffn_conv_w"]), "conv_b": per_feature(a["ffn_conv_b"]),
        "mix_g": per_feature(a["ln_mix_g"]), "mix_b": per_feature(a["ln_mix_b"]),
        "ffn_g": per_feature(a["ln_ffn_g"]), "ffn_b": per_feature(a["ln_ffn_b"]),
        "norm_g": per_feature(a["norm_g_2"]), "mem_g": per_feature(a["mem_norm_g_2"]),
        "pool_scale": per_feature(a["pool_scale_2"]),
        "fox_qg": twice(a["fox_q_g_2"][0]), "fox_kg": twice(a["fox_k_g_2"][0]),
        "mem_qg": twice(a["mem_q_g_2"][0]), "mem_kg": twice(a["mem_k_g_2"][0]),
        "forget_b": np.concatenate([a["b_f_2"][0], np.zeros(P - 8, np.float32)]).reshape(P, 1),
    }
    params = np.concatenate([vec[n] for n, _ in PARAMS], axis=1)
    rel_in = np.zeros((BUCKETS + SWH, SWH + 2 * P), np.float32)
    rel_in[0:BUCKETS, 0:SWH] = a["rel_bias"]
    rel_in[0:BUCKETS, SWH:] = hot
    rel_in[BUCKETS:, SWH:] = row_mask
    w_pool = np.zeros((P, 2, P), np.float32)
    for g in range(4):
        r = 64 * (g % 2)
        w_pool[r:r + 64, g // 2, r:r + 64] = a["w_pool_2"][0, g]
    arrays = {
        "stream": stream,
        "x_t": a["x"][0].reshape(T, KB, P).transpose(2, 1, 0),
        "mem_t": a["mem_2"][0].reshape(MEM, KB, P).transpose(2, 1, 0),
        "params": params, "consts": con, "masks": masks, "sinks": a["swa_sinks"].reshape(SWH),
        "rel_in": rel_in, "w_pool": w_pool,
    }
    arrays = {k: np.ascontiguousarray(v) for k, v in arrays.items()}
    nc = bacc.Bacc("TRN2", target_bir_lowering=False, num_devices=1)
    args = [nc.dram_tensor(k, v.shape, mybir.dt.from_np(v.dtype), kind="ExternalInput").ap() for k, v in arrays.items()]
    out = nc.dram_tensor("out", (P, KB, T), F32, kind="ExternalOutput").ap()
    build(nc, *args, out)
    r = run_bass_kernel_spmd(nc, [arrays], core_ids=[0])
    got = r.results[0]["out"]
    return np.ascontiguousarray(got.transpose(2, 1, 0)).reshape(1, T, D)
```
